# Optimizing a Trainium2 kernel written in Bass

```python
import math
import jax, jax.numpy as jnp
from jax import lax
import numpy as np

D_MODEL = 1024
BATCH = 1
SEQ = 1024
DEPTH = 1

D_MIX = D_MODEL
ATTN_WIDTH = D_MIX // 2
CONV_WIDTH = D_MIX - ATTN_WIDTH
DV = 128
N_ATTN_HEADS = ATTN_WIDTH // DV
DK = DV // 2
ROT_DIM = DK // 4
ROPE_THETA = 500000.0
Q_COLS = N_ATTN_HEADS * 2 * DK
K_COLS = N_ATTN_HEADS * 2 * DK
V_COLS = N_ATTN_HEADS * DV
IN_COLS = Q_COLS + K_COLS + V_COLS + 3 * CONV_WIDTH
CONV_K = 3
Q_BLOCK = 128
NORM_EPS = 1e-6
N_GROUPS = 4
EXPERTS_PER_GROUP = 8
N_EXPERTS = N_GROUPS * EXPERTS_PER_GROUP
TOP_K = 2
D_FF_EXPERT = D_MODEL // 2
MOE_BLOCK = 256

kernel_name = "hymba_diffattn_shortconv_hiermoe"

def rms_norm(x, gain, eps=NORM_EPS):
    xf = x.astype(jnp.float32)
    y = xf * lax.rsqrt(jnp.mean(xf * xf, axis=-1, keepdims=True) + eps)
    return (y * gain.astype(jnp.float32)).astype(x.dtype)

def partial_rotary(t, positions):
    half = ROT_DIM // 2
    freqs = ROPE_THETA ** (-jnp.arange(0, ROT_DIM, 2, dtype=jnp.float32) / ROT_DIM)
    ang = positions.astype(jnp.float32)[..., None] * freqs
    cos = jnp.cos(ang)[:, :, None, None, :]
    sin = jnp.sin(ang)[:, :, None, None, :]
    tf = t.astype(jnp.float32)
    t1, t2, rest = tf[..., :half], tf[..., half:ROT_DIM], tf[..., ROT_DIM:]
    out = jnp.concatenate([t1 * cos - t2 * sin, t2 * cos + t1 * sin, rest], axis=-1)
    return out.astype(t.dtype)

def diff_attention(q, k, v, lam, lambda_init, subln_gain):
    bsz, seq = q.shape[0], q.shape[1]
    scale = DK ** -0.5
    outs = []
    for i in range(seq // Q_BLOCK):
        q0 = i * Q_BLOCK
        end = q0 + Q_BLOCK
        qb = q[:, q0:end]
        kb = k[:, :end]
        vb = v[:, :end]
        s = jnp.einsum('bqhmd,bkhmd->bhmqk', qb, kb).astype(jnp.float32) * scale
        mask = jnp.arange(end)[None, :] <= (q0 + jnp.arange(Q_BLOCK))[:, None]
        s = jnp.where(mask, s, -jnp.inf)
        p = jax.nn.softmax(s, axis=-1)
        a = p[:, :, 0] - lam * p[:, :, 1]
        outs.append(jnp.einsum('bhqk,bkhd->bqhd', a.astype(v.dtype), vb))
    o = jnp.concatenate(outs, axis=1)
    o = rms_norm(o, subln_gain) * (1.0 - lambda_init)
    return o.reshape(bsz, seq, N_ATTN_HEADS * DV)

def short_conv(cb, cc, cu, conv_w, out_gain):
    y = cc * cu
    yp = jnp.pad(y, ((0, 0), (CONV_K - 1, 0), (0, 0)))
    seq = y.shape[1]
    z = sum(conv_w[j] * yp[:, j:j + seq] for j in range(CONV_K))
    return rms_norm(cb * z, out_gain)

def hier_moe(h, w_group_router, w_expert_router, w_gate, w_up, w_down):
    bsz, seq, d = h.shape
    xf = h.reshape(-1, d)
    n_tok = xf.shape[0]
    g_logits = (xf @ w_group_router).astype(jnp.float32)
    g_prob = jax.nn.softmax(g_logits, axis=-1)
    g_sel = jnp.argmax(g_logits, axis=-1)
    g_gate = jnp.take_along_axis(g_prob, g_sel[:, None], axis=-1)
    e_logits = jnp.einsum('nd,gde->nge', xf, w_expert_router).astype(jnp.float32)
    e_sel = jnp.take_along_axis(e_logits, g_sel[:, None, None], axis=1)[:, 0]
    top_v, top_i = lax.top_k(e_sel, TOP_K)
    weights = jax.nn.softmax(top_v, axis=-1) * g_gate
    expert_id = g_sel[:, None] * EXPERTS_PER_GROUP + top_i

    n_assign = n_tok * TOP_K
    flat_e = expert_id.reshape(-1)
    flat_w = weights.reshape(-1)
    flat_t = jnp.repeat(jnp.arange(n_tok, dtype=jnp.int32), TOP_K)
    order = jnp.argsort(flat_e)
    se, st, sw = flat_e[order], flat_t[order], flat_w[order]
    counts = jnp.bincount(flat_e, length=N_EXPERTS)
    starts = jnp.cumsum(counts) - counts
    padded = ((counts + MOE_BLOCK - 1) // MOE_BLOCK) * MOE_BLOCK
    pad_ends = jnp.cumsum(padded)
    pad_starts = pad_ends - padded
    dest = pad_starts[se] + (jnp.arange(n_assign) - starts[se])
    n_blocks = -(-n_assign // MOE_BLOCK) + N_EXPERTS
    rows = jnp.zeros((n_blocks * MOE_BLOCK, d), xf.dtype).at[dest].set(xf[st])
    block_start = jnp.arange(n_blocks) * MOE_BLOCK
    block_e = jnp.minimum(jnp.sum(pad_ends[None, :] <= block_start[:, None], axis=1), N_EXPERTS - 1)

    def expert_block(args):
        xb, e = args
        return (jax.nn.silu(xb @ w_gate[e]) * (xb @ w_up[e])) @ w_down[e]

    out_rows = lax.map(expert_block, (rows.reshape(n_blocks, MOE_BLOCK, d), block_e))
    out_rows = out_rows.reshape(n_blocks * MOE_BLOCK, d)
    y_assign = out_rows[dest] * sw[:, None].astype(out_rows.dtype)
    y = jax.ops.segment_sum(y_assign, st, num_segments=n_tok)
    return y.reshape(bsz, seq, d)

def setup_inputs(seed: int = 0) -> dict:
    key = jax.random.key(seed)
    ks = jax.random.split(key, 24)
    f32 = jnp.float32

    def nrm(k, shape, scale):
        return jax.random.normal(k, shape, f32) * scale

    def gain(k, shape):
        return 1.0 + 0.02 * jax.random.normal(k, shape, f32)

    x = jax.random.normal(ks[0], (BATCH, SEQ, D_MODEL), f32)
    offsets = jax.random.randint(ks[1], (BATCH, 1), 0, 1024, dtype=jnp.int32)
    positions = (offsets + jnp.arange(SEQ, dtype=jnp.int32)[None, :]).astype(jnp.int32)
    return {
        "x": x,
        "positions": positions,
        "attn_norm_gain": gain(ks[2], (DEPTH, D_MODEL)),
        "w_in": nrm(ks[3], (DEPTH, D_MODEL, IN_COLS), D_MODEL ** -0.5),
        "q_norm_gain": gain(ks[4], (DEPTH, DK)),
        "k_norm_gain": gain(ks[5], (DEPTH, DK)),
        "lambda_q1": nrm(ks[6], (DEPTH, DK), 0.1),
        "lambda_k1": nrm(ks[7], (DEPTH, DK), 0.1),
        "lambda_q2": nrm(ks[8], (DEPTH, DK), 0.1),
        "lambda_k2": nrm(ks[9], (DEPTH, DK), 0.1),
        "subln_gain": gain(ks[10], (DEPTH, DV)),
        "conv_w": nrm(ks[11], (DEPTH, CONV_K, CONV_WIDTH), CONV_K ** -0.5),
        "conv_out_gain": gain(ks[12], (DEPTH, CONV_WIDTH)),
        "w_out": nrm(ks[13], (DEPTH, D_MIX, D_MODEL), D_MIX ** -0.5),
        "ffn_norm_gain": gain(ks[14], (DEPTH, D_MODEL)),
        "w_group_router": nrm(ks[15], (DEPTH, D_MODEL, N_GROUPS), D_MODEL ** -0.5),
        "w_expert_router": nrm(ks[16], (DEPTH, N_GROUPS, D_MODEL, EXPERTS_PER_GROUP), D_MODEL ** -0.5),
        "w_gate": nrm(ks[17], (DEPTH, N_EXPERTS, D_MODEL, D_FF_EXPERT), D_MODEL ** -0.5),
        "w_up": nrm(ks[18], (DEPTH, N_EXPERTS, D_MODEL, D_FF_EXPERT), D_MODEL ** -0.5),
        "w_down": nrm(ks[19], (DEPTH, N_EXPERTS, D_FF_EXPERT, D_MODEL), D_FF_EXPERT ** -0.5),
    }

def reference(x, positions, attn_norm_gain, w_in, q_norm_gain, k_norm_gain,
              lambda_q1, lambda_k1, lambda_q2, lambda_k2, subln_gain, conv_w,
              conv_out_gain, w_out, ffn_norm_gain, w_group_router, w_expert_router,
              w_gate, w_up, w_down):
    bsz, seq, _ = x.shape
    splits = [Q_COLS, Q_COLS + K_COLS, Q_COLS + K_COLS + V_COLS,
              Q_COLS + K_COLS + V_COLS + CONV_WIDTH,
              Q_COLS + K_COLS + V_COLS + 2 * CONV_WIDTH]
    for l in range(DEPTH):
        lambda_init = 0.8 - 0.6 * math.exp(-0.3 * l)
        hn = rms_norm(x, attn_norm_gain[l])
        proj = hn @ w_in[l]
        q, k, v, cb, cc, cu = jnp.split(proj, splits, axis=-1)
        q = q.reshape(bsz, seq, N_ATTN_HEADS, 2, DK)
        k = k.reshape(bsz, seq, N_ATTN_HEADS, 2, DK)
        v = v.reshape(bsz, seq, N_ATTN_HEADS, DV)
        q = partial_rotary(rms_norm(q, q_norm_gain[l]), positions)
        k = partial_rotary(rms_norm(k, k_norm_gain[l]), positions)
        lam = (jnp.exp(jnp.sum(lambda_q1[l].astype(jnp.float32) * lambda_k1[l].astype(jnp.float32)))
               - jnp.exp(jnp.sum(lambda_q2[l].astype(jnp.float32) * lambda_k2[l].astype(jnp.float32)))
               + lambda_init)
        attn_o = diff_attention(q, k, v, lam, lambda_init, subln_gain[l])
        conv_o = short_conv(cb, cc, cu, conv_w[l], conv_out_gain[l])
        x = x + jnp.concatenate([attn_o, conv_o], axis=-1) @ w_out[l]
        hn2 = rms_norm(x, ffn_norm_gain[l])
        x = x + hier_moe(hn2, w_group_router[l], w_expert_router[l],
                         w_gate[l], w_up[l], w_down[l])
    return x


_drawn_inputs = setup_inputs


def setup_inputs(seed=0):
    import zlib

    import numpy as np

    out = dict(_drawn_inputs(seed))
    spreads = {}
    factors = {'q_norm_gain': 3.172,
     'k_norm_gain': 3.496,
     'lambda_q1': 2.882,
     'lambda_k2': 6.07,
     'subln_gain': 11.991,
     'conv_out_gain': 10.747,
     'ffn_norm_gain': 6.108}
    for name, (base, spread) in spreads.items():
        noise = np.random.default_rng([zlib.crc32(name.encode()), seed]).standard_normal(out[name].shape)
        drawn = base * np.exp(spread * noise) if base else spread * noise
        out[name] = __import__('jax').numpy.asarray(drawn.astype(out[name].dtype))
    for name, factor in factors.items():
        out[name] = (out[name] * factor).astype(out[name].dtype)
    return out
```

```python
from contextlib import ExitStack

import concourse.bass as bass
from concourse import mybir

F32 = mybir.dt.float32
F32R = mybir.dt.float32r
BF16 = mybir.dt.bfloat16
U32 = mybir.dt.uint32
I32 = mybir.dt.int32
ALU = mybir.AluOpType
ACT = mybir.ActivationFunctionType
AX = mybir.AxisListType

P = 128
T = 1024
D = 1024
NT = T // P
KC = D // P
HEADS = 4
DV = 128
DK = 64
CONV = 512
CT = CONV // P
ROT = 16
THETA = 500000.0
EPS = 1e-6
GROUPS = 4
PER_GROUP = 8
E = GROUPS * PER_GROUP
FF = 512
FC = FF // P
TOP_K = 2
COL_Q, COL_K, COL_V, COL_B, COL_C, COL_U = 0, 512, 1024, 1536, 2048, 2560
LAMBDA_INIT = 0.2
MASKED = -1e30
SPARE = (T * TOP_K - E) // P
BLOCKS = E + SPARE
NO_TOKEN = T

KB = 1024


class Shared:
    pass


class Order:

    def __init__(self, eng, sem):
        self.eng, self.sem, self.n, self.start, self.i, self.steps = eng, sem, 0, 0, None, 0

    def value(self, n):
        return self.start + n if self.i is None else self.i * self.steps + (self.start + n)

    def mark(self, ins):
        ins.then_inc(self.sem, 1)
        self.n += 1
        return self.n

    def wait(self, n):
        self.eng.wait_ge(self.sem, self.value(n))

    def then(self, ins):
        self.wait(self.mark(ins))

    def enter(self, i, steps):
        self.start, self.n, self.i, self.steps = self.start + self.n, 0, i, steps

    def leave(self, times):
        assert self.n == self.steps, (self.n, self.steps)
        self.start, self.n, self.i = self.start + times * self.steps, 0, None


def layer_kernel(nc, x, positions, attn_norm_gain, w_in, q_norm_gain, k_norm_gain, lambda_q1,
                 lambda_k1, lambda_q2, lambda_k2, subln_gain, conv_w, conv_out_gain, w_out,
                 ffn_norm_gain, w_group_router, w_expert_router, w_gate, w_up, w_down, out):
    ctx = ExitStack()
    with ctx:
        base = nc.sbuf_base
        slab = 207 * KB
        ctx.enter_context(nc.sbuf_tensor("slab", [P, slab], mybir.dt.uint8))
        base = -(-base // 32) * 32

        def at(name, kb, shape, dtype=F32):
            return nc.alloc_sbuf_tensor_at(name, shape, dtype, offset=base + int(kb * KB))

        ps = ctx.enter_context(nc.psum_tensor("banks", [P, 8, 512], F32))

        def sem(name):
            return ctx.enter_context(nc.semaphore(name))

        xn2_rows = nc.dram_tensor("xn2_rows", [T, D], F32, kind="Internal").ap()
        table_rows = nc.dram_tensor("table_rows", [P * BLOCKS, 2], U32, kind="Internal").ap()

        out_rows = out.rearrange("b t d -> (b t) d")
        x_rows = x.rearrange("b t d -> (b t) d")

        ident = at("ident", 0, [P, P])
        ident_b = at("ident_b", 0.5, [P, P], BF16)
        causal_b = at("causal_b", 0.75, [P, P], BF16)
        before_b = at("before_b", 1, [P, P], BF16)
        ones_b = at("ones_b", 1.25, [P, P], BF16)
        cos2 = at("cos2", 1.5, [P, NT, ROT])
        sin2 = at("sin2", 2, [P, NT, ROT])
        qk_gain = at("qk_gain", 2.5, [P, 2, 2, DK])
        conv_taps = at("conv_taps", 3.5, [P, CT, 4])
        sub_gain = at("sub_gain", 3.625, [P, 1])
        neg_lam = at("neg_lam", 3.65625, [P, 1])
        neg_half = at("neg_half", 3.6875, [P, NT])
        ones_col = at("ones_col", 3.71875, [P, 1])
        eps_qk = at("eps_qk", 3.75, [P, NT])
        eps_o = at("eps_o", 3.78125, [P, 1])
        rstd_c = at("rstd_c", 4, [P, NT])
        pos_i = at("pos_i", 4.03125, [P, NT], I32)
        rstd_x = at("rstd_x", 4.0625, [P, NT])
        ss_x = at("ss_x", 4.09375, [P, NT])
        ang = at("ang", 4.125, [P, NT, 8])
        angc = at("angc", 4.375, [P, NT, 8])
        turns = at("turns", 4.625, [P, NT, 8])
        lam4 = at("lam4", 5, [P, 4, DK])
        lamt = at("lamt", 6, [P, DK])
        posf = at("posf", 6.25, [P, NT])
        freqs = at("freqs", 6.3125, [P, 8])
        lamd = at("lamd", 6.375, [P, 4])

        xT_hi = at("xT_hi", 8, [P, KC, T], F32R)
        xT_lo = at("xT_lo", 40, [P, KC, T], F32R)
        mixT = at("mixT", 72, [P, KC, T])

        x_all = at("x_all", 104, [P, NT, D])
        xn = [at(f"xn{b}", 136 + 4 * b, [P, D]) for b in range(2)]
        gain1 = at("gain1", 144, [P, D])
        squares = at("squares", 148, [P, D])

        z_raw = [at(f"z_raw{s}", 160 + 4 * s, [P, KC, P]) for s in range(2)]
        z_hi = [at(f"z_hi{s}", 168 + 4 * s, [P, KC, P], F32R) for s in range(2)]
        z_lo = [at(f"z_lo{s}", 176 + 4 * s, [P, KC, P], F32R) for s in range(2)]
        c_sb = at("c_sb", 184, [P, T])
        cu = at("cu", 188, [P, T + 2])
        z_taps = at("z_taps", 193, [P, 4])

        q_raw = at("q_raw", 104, [P, KC, 3, P])
        b_raw = at("b_raw", 116, [P, KC, P])
        q_hi = at("q_hi", 120, [P, KC, 3 * P], F32R)
        q_lo = at("q_lo", 132, [P, KC, 3 * P], F32R)
        b_hi = at("b_hi", 144, [P, KC, P], F32R)
        b_lo = at("b_lo", 148, [P, KC, P], F32R)
        q_stack = at("q_stack", 152, [P, 2, T], F32R)
        k_hi = at("k_hi", 160, [P, 2, T], F32R)
        k_lo = at("k_lo", 168, [P, 2, T], F32R)
        v_sb = at("v_sb", 176, [P, NT, DV])
        probs = [at("probs0", 180, [P, 2, T - P]), at("probs1", 187, [P, 2, T])]
        mapsT = [at("mapsT0", 195, [P, NT - 1, P]), at("mapsT1", 198.5, [P, NT, P])]
        conv_sq = at("conv_sq", 202.5, [P, T])
        qk_scaled = [at(f"qk_scaled{b}", 180 + b, [P, 4, DK]) for b in range(2)]
        qk_twice = [at(f"qk_twice{b}", 182 + 2 * b, [P, 4, 2, DK]) for b in range(2)]
        rot_a = at("rot_a", 186, [P, 4, ROT])
        rot_b = at("rot_b", 186.25, [P, 4, ROT])
        qk_sq = at("qk_sq", 186.5, [P, 4, DK])
        bz = at("bz", 188, [P, T])
        bz_sq = at("bz_sq", 195, [P, T])
        g_taps = at("g_taps", 206.5, [P, 4])
        qk_ss = at("qk_ss", 206.53125, [P, 2, 4])
        qk_rstd = at("qk_rstd", 206.5625, [P, 2, 4])
        neg_max = at("neg_max", 206.59375, [P, 2, 2])
        sums = at("sums", 206.625, [P, 8, 2])
        inv_sums = at("inv_sums", 206.6875, [P, 8, 2])
        ratio = at("ratio", 206.75, [P, 2])
        o_ss = at("o_ss", 206.78125, [P, 2])
        o_rstd = at("o_rstd", 206.8125, [P, 2])
        o_sb = [at(f"o_sb{b}", 6.5 + 0.5 * b, [P, DV]) for b in range(2)]
        o_sq = at("o_sq", 5, [P, DV])

        wo_hi = at("wo_hi", 8, [P, KC, D], F32R)
        wo_lo = at("wo_lo", 40, [P, KC, D], F32R)
        wo_raw = [at(f"wo_raw{b}", 104 + 4 * b, [P, D]) for b in range(2)]
        m_hi = [at(f"m_hi{b}", 112 + 4 * b, [P, KC, P], F32R) for b in range(2)]
        m_lo = [at(f"m_lo{b}", 120 + 4 * b, [P, KC, P], F32R) for b in range(2)]
        x_again = [at(f"x_again{b}", 128 + 4 * b, [P, D]) for b in range(2)]
        h_sb = [at(f"h_sb{b}", 136 + 4 * b, [P, D]) for b in range(2)]
        hn = [at(f"hn{b}", 144 + 4 * b, [P, KC, P]) for b in range(2)]
        hnT = at("hnT", 152, [P, KC, P])
        h_sq = at("h_sq", 156, [P, D])
        gain2 = at("gain2", 160, [P, D])
        w_route = at("w_route", 164, [P, KC, GROUPS + E])
        logits = at("logits", 166, [P, NT, GROUPS + E])
        h_ss = at("h_ss", 168, [P, 2])
        h_rstd = at("h_rstd", 168.0625, [P, 2])

        raw = [[at(f"raw{b}_{k}", 8 + 8 * (6 * b + k), [P, 2048]) for k in range(6)] for b in range(2)]
        w_lo = [[at(f"wlo{b}_{k}", 8 + 8 * (6 * b + k), [P, 2048], F32R) for k in range(6)]
                for b in range(2)]
        w_hi = [at(f"whi{k}", 104 + 8 * k, [P, 2048], F32R) for k in range(6)]
        rows = [at(f"rows{b}", 152 + 4 * b, [P, KC, P]) for b in range(2)]
        rT_hi = [at(f"rT_hi{b}", 160 + 4 * b, [P, KC, P], F32R) for b in range(2)]
        rT_lo = [at(f"rT_lo{b}", 168 + 4 * b, [P, KC, P], F32R) for b in range(2)]
        hid = [at(f"hid{b}", 176 + 2 * b, [P, FC, P]) for b in range(2)]
        hidT_hi = at("hidT_hi", 180, [P, FC, P], F32R)
        hidT_lo = at("hidT_lo", 182, [P, FC, P], F32R)
        silu = at("silu", 184, [P, FF])
        y_sb = [at(f"y_sb{b}", 186 + 4 * b, [P, D]) for b in range(2)]
        table = at("table", 194, [P, BLOCKS, 2], U32)
        spare_xT = at("spare_xT", 195, [P, KC, P])
        spare_hT = at("spare_hT", 199, [P, FC, P])
        idx_g = [at(f"idx_g{b}", 201 + 0.0625 * b, [P, 1], U32) for b in range(2)]
        idx_s = [at(f"idx_s{b}", 201.125 + 0.0625 * b, [P, 1], U32) for b in range(2)]
        w_slot = [at(f"w_slot{b}", 201.25 + 0.0625 * b, [P, 1]) for b in range(2)]
        spare_n = at("spare_n", 201.5, [P, 1], I32)
        spare_e = at("spare_e", 201.5625, [P, SPARE], I32)

        small_in = sem("small_in")
        gain1_in = sem("gain1_in")
        x_in = [sem(f"x_in{t}") for t in range(NT // 2)]
        z_raw_in = [sem(f"z_raw_in{s}") for s in range(2)]
        consts = sem("consts")
        squared = sem("squared")
        pool_own = sem("pool_own")
        dve_own = sem("dve_own")
        rstd_ready = sem("rstd_ready")
        xn_ready = sem("xn_ready")
        xn_turned = sem("xn_turned")
        xhi_ready = sem("xhi_ready")
        xlo_ready = sem("xlo_ready")
        angles_ready = sem("angles_ready")
        tables_ready = sem("tables_ready")
        lam_dots = sem("lam_dots")
        lam_exp = sem("lam_exp")
        w_in_pc = w_in[0].rearrange("(c p) n -> p c n", p=P)

        with nc.Block() as block:
            @block.sync
            def _(sp):
                for t in range(0, NT, 2):
                    sp.dma_start(x_all[:, t:t + 2, :], x_rows[t * P:(t + 2) * P, :].rearrange("(a p) d -> p a d", p=P)).then_inc(x_in[t // 2], 16)
                sp.dma_start(gain1[:], attn_norm_gain[0:1, :].to_broadcast([P, D])).then_inc(gain1_in, 16)
                for s, col in ((0, COL_C), (1, COL_U)):
                    sp.dma_start(z_raw[s][:], w_in_pc[:, :, col:col + P]).then_inc(z_raw_in[s], 16)

            @block.gpsimd
            def _(pool):
                own = Order(pool, pool_own)
                with nc.allow_non_contiguous_dma(reason="positions and gains, a few hundred words"):
                    pool.dma_start(pos_i[:], positions[0].rearrange("(t p) -> p t", p=P)).then_inc(small_in, 16)
                    for m, g in enumerate((q_norm_gain, k_norm_gain)):
                        for n in range(2):
                            pool.dma_start(qk_gain[:, m, n, :], g[0:1, :].to_broadcast([P, DK])).then_inc(small_in, 16)
                    for j, g in enumerate((lambda_q1, lambda_k1, lambda_q2, lambda_k2)):
                        pool.dma_start(lam4[:, j, :], g[0:1, :].to_broadcast([P, DK])).then_inc(small_in, 16)
                    for m in range(CT):
                        pool.dma_start(conv_taps[:, m, 0:3], conv_w[0][:, m * P:(m + 1) * P].rearrange("j p -> p j")).then_inc(small_in, 16)
                    pool.dma_start(conv_taps[:, :, 3], conv_out_gain[0].rearrange("(m p) -> p m", p=P)).then_inc(small_in, 16)
                    pool.dma_start(sub_gain[:], subln_gain.rearrange("a p -> p a")).then_inc(small_in, 16)
                pool.memset(neg_half[:], -0.5).then_inc(consts, 1)
                pool.memset(ones_col[:], 1.0).then_inc(consts, 1)
                pool.memset(eps_qk[:], EPS).then_inc(consts, 1)
                pool.memset(eps_o[:], EPS * DV).then_inc(consts, 1)
                pool.memset(conv_sq[:], 0.0).then_inc(consts, 1)
                pool.memset(ones_b[:], 1.0).then_inc(consts, 1)
                own.mark(pool.memset(ident[:], 0.0))
                own.mark(pool.memset(ident_b[:], 0.0))
                own.mark(pool.memset(causal_b[:], 0.0))
                own.then(pool.memset(before_b[:], 1.0))
                pool.affine_select(out=ident[:], in_=ident[:], compare_op=ALU.not_equal, fill=1.0, base=0,
                                   pattern=[[-1, P]], channel_multiplier=1).then_inc(consts, 1)
                pool.affine_select(out=ident_b[:], in_=ident_b[:], compare_op=ALU.not_equal, fill=1.0, base=0,
                                   pattern=[[-1, P]], channel_multiplier=1).then_inc(consts, 1)
                pool.affine_select(out=causal_b[:], in_=causal_b[:], compare_op=ALU.is_ge, fill=MASKED, base=0,
                                   pattern=[[-1, P]], channel_multiplier=1).then_inc(consts, 1)
                pool.affine_select(out=before_b[:], in_=before_b[:], compare_op=ALU.is_gt, fill=0.0, base=0,
                                   pattern=[[1, P]], channel_multiplier=-1).then_inc(consts, 1)
                pool.wait_ge(squared, NT)
                own.then(pool.tensor_scalar(ss_x[:], ss_x[:], 1.0 / D, EPS, ALU.mult, ALU.add))
                pool.tensor_tensor(rstd_x[:], ss_x[:], neg_half[:], ALU.pow).then_inc(rstd_ready, 1)

            @block.scalar
            def _(act):
                for t in range(NT):
                    act.wait_ge(x_in[t // 2], 16)
                    act.activation(squares[:], x_all[:, t, :], ACT.Square,
                                   accum_out=ss_x[:, t:t + 1]).then_inc(squared, 1)
                    act.wait_ge(squared, t + 1)
                act.wait_ge(angles_ready, 1)
                act.activation(sin2[:, :, 8:16], ang[:], ACT.Sin).then_inc(tables_ready, 1)
                act.activation(cos2[:, :, 0:8], angc[:], ACT.Sin).then_inc(tables_ready, 1)
                act.wait_ge(lam_dots, 1)
                act.activation(lamd[:, 2:4], lamd[:, 0:2], ACT.Exp).then_inc(lam_exp, 1)
                with act.Fori(0, NT // 2) as j:
                    for b in range(2):
                        act.wait_ge(xn_turned, j * 2 + (b + 1))
                        act.copy(xT_hi[:, :, bass.ds((j * 2 + b) * P, P)].rearrange("p (a c) q -> p a c q", a=2),
                                 ps[:, 2 * b:2 * b + 2, :].rearrange("p a (c q) -> p a c q", q=P)).then_inc(xhi_ready, 1)

            @block.vector
            def _(dve):
                own = Order(dve, dve_own)
                own.mark(dve.memset(cu[:, 0:2], 0.0))
                for j in range(8):
                    own.mark(dve.memset(freqs[:, j:j + 1], float(THETA) ** (-(2 * j) / ROT)))
                dve.wait_ge(small_in, 16 * 15)
                own.mark(dve.tensor_scalar(qk_gain[:, 0, :, :], qk_gain[:, 0, :, :], DK ** -0.5, None, ALU.mult))
                own.mark(dve.tensor_scalar(sub_gain[:], sub_gain[:], (1.0 - LAMBDA_INIT) * DV ** 0.5, None, ALU.mult))
                own.then(dve.tensor_copy(posf[:], pos_i[:]))
                own.then(dve.tensor_tensor(ang[:], posf[:].unsqueeze(2).to_broadcast([P, NT, 8]),
                                           freqs[:].unsqueeze(1).to_broadcast([P, NT, 8]), ALU.mult))
                ROUND = 12582912.0
                TWO_PI = (6.28125, 1.93500518798828125e-3, 3.0199159819567e-7)
                own.then(dve.tensor_scalar(turns[:], ang[:], 0.15915494309189535, 0.25, ALU.mult, ALU.add))
                own.then(dve.tensor_scalar(turns[:], turns[:], ROUND, None, ALU.add))
                own.then(dve.tensor_scalar(turns[:], turns[:], -ROUND, None, ALU.add))
                own.then(dve.scalar_tensor_tensor(angc[:], turns[:], -TWO_PI[0], ang[:], ALU.mult, ALU.add))
                for part in TWO_PI[1:]:
                    own.then(dve.scalar_tensor_tensor(angc[:], turns[:], -part, angc[:], ALU.mult, ALU.add))
                own.then(dve.tensor_scalar(angc[:], angc[:], 1.5707963267948966, 3.1415925, ALU.add, ALU.min))
                own.then(dve.tensor_scalar(angc[:], angc[:], -3.1415925, None, ALU.max))
                own.then(dve.tensor_scalar(turns[:], ang[:], 0.15915494309189535, None, ALU.mult))
                own.then(dve.tensor_scalar(turns[:], turns[:], ROUND, None, ALU.add))
                own.then(dve.tensor_scalar(turns[:], turns[:], -ROUND, None, ALU.add))
                for part in TWO_PI:
                    own.then(dve.scalar_tensor_tensor(ang[:], turns[:], -part, ang[:], ALU.mult, ALU.add))
                dve.tensor_scalar(ang[:], ang[:], 3.1415925, -3.1415925, ALU.min, ALU.max).then_inc(angles_ready, 1)
                own.then(dve.tensor_tensor_reduce(lamt[:], lam4[:, 0, :], lam4[:, 1, :], 1.0, 0.0, ALU.mult, ALU.add, lamd[:, 0:1]))
                dve.tensor_tensor_reduce(lamt[:], lam4[:, 2, :], lam4[:, 3, :], 1.0, 0.0, ALU.mult, ALU.add, lamd[:, 1:2]).then_inc(lam_dots, 1)
                dve.wait_ge(lam_exp, 1)
                own.then(dve.tensor_tensor(neg_lam[:], lamd[:, 3:4], lamd[:, 2:3], ALU.subtract))
                own.mark(dve.tensor_scalar(neg_lam[:], neg_lam[:], -LAMBDA_INIT, None, ALU.add))
                dve.wait_ge(tables_ready, 2)
                own.mark(dve.tensor_copy(cos2[:, :, 8:16], cos2[:, :, 0:8]))
                own.then(dve.tensor_scalar(sin2[:, :, 0:8], sin2[:, :, 8:16], -1.0, None, ALU.mult))
                dve.wait_ge(gain1_in, 16)
                dve.wait_ge(rstd_ready, 1)

                def scale(t, b):
                    dve.scalar_tensor_tensor(xn[b][:], x_all[:, t, :], rstd_x[:, t:t + 1], gain1[:],
                                             ALU.mult, ALU.mult).then_inc(xn_ready, 1)

                for t in range(NT):
                    if t >= 2:
                        dve.wait_ge(xn_turned, t - 1)
                    scale(t, t % 2)
                    if t >= 1:
                        low_half(nc, dve, t - 1, xhi_ready, xT_hi, xT_lo, ps, xlo_ready)
                low_half(nc, dve, NT - 1, xhi_ready, xT_hi, xT_lo, ps, xlo_ready)

            @block.tensor
            def _(pe):
                pe.wait_ge(consts, 10)
                for t in range(NT):
                    b = t % 2
                    pe.wait_ge(xn_ready, t + 1)
                    if t >= 2:
                        pe.wait_ge(xlo_ready, t - 1)
                    for c in range(KC):
                        ins = pe.transpose(ps[:, 2 * b + c // 4, (c % 4) * P:(c % 4 + 1) * P],
                                           xn[b][:, c * P:(c + 1) * P], ident[:])
                    ins.then_inc(xn_turned, 1)

        z_hi_ready = [sem(f"z_hi_ready{s}") for s in range(2)]
        z_lo_ready = [sem(f"z_lo_ready{s}") for s in range(2)]
        z_multiplied = [sem(f"z_multiplied{s}") for s in range(2)]
        c_copied = sem("c_copied")
        cu_ready = sem("cu_ready")
        q_in = sem("q_in")
        b_in = sem("b_in")
        dve_own2 = sem("dve_own2")

        def load_head(sp, h):
            for j, col in enumerate((COL_Q, COL_K, COL_V)):
                sp.dma_start(q_raw[:, :, j, :], w_in_pc[:, :, bass.ds(h * P + col, P)]).then_inc(q_in, 16)
            sp.dma_start(b_raw[:], w_in_pc[:, :, bass.ds(h * P + COL_B, P)]).then_inc(b_in, 16)

        with nc.Block() as block:
            @block.sync
            def _(sp):
                load_head(sp, 0)
                with sp.Fori(0, CT - 1) as m:
                    for s, col in ((0, COL_C), (1, COL_U)):
                        sp.wait_ge(z_lo_ready[s], m + 1)
                        sp.dma_start(z_raw[s][:], w_in_pc[:, :, bass.ds(m * P + (col + P), P)]).then_inc(z_raw_in[s], 16)

            @block.scalar
            def _(act):
                with act.Fori(0, CT) as m:
                    for s in range(2):
                        act.wait_ge(z_raw_in[s], m * 16 + 16)
                        act.wait_ge(z_multiplied[s], m + 1)
                        act.copy(z_hi[s][:], z_raw[s][:]).then_inc(z_hi_ready[s], 1)
                    act.wait_ge(z_multiplied[0], m + 2)
                    act.wait_ge(cu_ready, m + 1)
                    act.copy(c_sb[:], ps[:, 0:2, :]).then_inc(c_copied, 1)

            @block.gpsimd
            def _(pool):
                with pool.Fori(0, CT) as m:
                    for s in range(2):
                        pool.wait_ge(z_hi_ready[s], m + 1)
                        pool.tensor_tensor(z_lo[s][:], z_raw[s][:], z_hi[s][:].bitcast(F32),
                                           ALU.subtract).then_inc(z_lo_ready[s], 1)

            @block.vector
            def _(dve):
                own = Order(dve, dve_own2)
                dve.sem_inc(cu_ready, 1)
                with dve.Fori(0, CT) as m:
                    own.enter(m, 4)
                    own.mark(dve.tensor_copy(z_taps[:], conv_taps[:, bass.ds(m, 1), :]))
                    dve.wait_ge(c_copied, m + 2)
                    dve.wait_ge(z_multiplied[1], m + 2)
                    dve.tensor_tensor(cu[:, 2:T + 2].rearrange("p (a n) -> p a n", a=2), ps[:, 2:4, :],
                                      c_sb[:].rearrange("p (a n) -> p a n", a=2), ALU.mult).then_inc(cu_ready, 1)
                    dve.wait_ge(cu_ready, m + 2)
                    own.wait(1)
                    z = mixT[:, bass.ds(m + HEADS, 1), :].rearrange("p a t -> p (a t)")
                    own.then(dve.tensor_scalar(z, cu[:, 0:T], z_taps[:, 0:1], None, ALU.mult))
                    own.then(dve.scalar_tensor_tensor(z, cu[:, 1:T + 1], z_taps[:, 1:2], z, ALU.mult, ALU.add))
                    own.then(dve.scalar_tensor_tensor(z, cu[:, 2:T + 2], z_taps[:, 2:3], z, ALU.mult, ALU.add))
                    own.leave(CT)

            @block.tensor
            def _(pe):
                for s in range(2):
                    pe.sem_inc(z_multiplied[s], 1)
                pe.sem_inc(c_copied, 1)
                with pe.Fori(0, CT) as m:
                    for s in range(2):
                        pe.wait_ge(z_lo_ready[s], m + 1)
                        if s == 0:
                            pe.wait_ge(c_copied, m + 1)
                        else:
                            pe.wait_ge(cu_ready, m + 1)
                        ins = product_T(pe, ps, 2 * s, z_hi[s], z_lo[s], xT_hi, xT_lo)
                        ins.then_inc(z_multiplied[s], 1)

        loaded = [[sem(f"loaded{b}_{k}") for k in range(6)] for b in range(2)]

        def load_gate_up(eng, e, b, q, done=None):
            slot = raw[b][q][:].rearrange("p (g c n) -> p g c n", g=2, c=2)
            for g, w in enumerate((w_gate, w_up)):
                rows_of = w[0, bass.ds(e, 1)].rearrange("a (p c) n -> p (a c) n", c=KC)
                eng.dma_start(slot[:, g, :, :], rows_of[:, 2 * q:2 * q + 2, :]).then_inc(done or loaded[b][q], 16)

        def load_down(eng, e, b, q, done=None):
            rows_of = w_down[0, bass.ds(e, 1)].rearrange("a (p c) n -> p (a c) n", c=FC)
            eng.dma_start(raw[b][4 + q][:].rearrange("p (c n) -> p c n", c=2),
                          rows_of[:, 2 * q:2 * q + 2, :]).then_inc(done or loaded[b][4 + q], 16)

        s = Shared()
        s.ps, s.load_head, s.b_in, s.b_hi, s.b_raw = ps, load_head, b_in, b_hi, b_raw
        s.q_in, s.q_hi, s.q_raw, s.qk_sq, s.v_sb = q_in, q_hi, q_raw, qk_sq, v_sb
        s.q_stack, s.k_hi, s.mapsT, s.probs, s.neg_max = q_stack, k_hi, mapsT, probs, neg_max
        s.sums, s.o_sq, s.inv_sums, s.o_ss, s.mixT = sums, o_sq, inv_sums, o_ss, mixT
        s.sub_gain, s.b_lo, s.q_lo, s.bz_sq, s.bz = sub_gain, b_lo, q_lo, bz_sq, bz
        s.conv_sq, s.qk_rstd, s.qk_ss, s.eps_qk, s.neg_half = conv_sq, qk_rstd, qk_ss, eps_qk, neg_half
        s.qk_twice, s.rot_a, s.cos2, s.rot_b, s.sin2 = qk_twice, rot_a, cos2, rot_b, sin2
        s.o_rstd, s.eps_o, s.g_taps, s.conv_taps, s.qk_scaled = o_rstd, eps_o, g_taps, conv_taps, qk_scaled
        s.qk_gain, s.k_lo, s.ratio, s.neg_lam, s.o_sb = qk_gain, k_lo, ratio, neg_lam, o_sb
        s.xT_hi, s.xT_lo, s.ident, s.ident_b, s.causal_b = xT_hi, xT_lo, ident, ident_b, causal_b
        s.w_out, s.wo_raw, s.x_again, s.x_rows, s.gain2 = w_out, wo_raw, x_again, x_rows, gain2
        s.ffn_norm_gain, s.out_rows, s.h_sb, s.xn2_rows, s.hn = ffn_norm_gain, out_rows, h_sb, xn2_rows, hn
        s.w_route, s.w_group_router, s.w_expert_router, s.rstd_c, s.h_rstd = w_route, w_group_router, w_expert_router, rstd_c, h_rstd
        s.h_ss, s.m_hi, s.wo_hi, s.h_sq, s.hnT = h_ss, m_hi, wo_hi, h_sq, hnT
        s.logits, s.m_lo, s.wo_lo, s.ones_col, s.at = logits, m_lo, wo_lo, ones_col, at
        s.load_gate_up, s.load_down, s.rows, s.spare_n, s.spare_e = load_gate_up, load_down, rows, spare_n, spare_e
        s.table, s.before_b, s.ones_b, s.loaded, s.w_hi = table, before_b, ones_b, loaded, w_hi
        s.raw, s.w_lo, s.idx_g, s.idx_s, s.y_sb = raw, w_lo, idx_g, idx_s, y_sb
        s.hidT_hi, s.rT_hi, s.silu, s.hidT_lo, s.rT_lo = hidT_hi, rT_hi, silu, hidT_lo, rT_lo
        s.w_slot, s.hid, s.spare_xT, s.spare_hT = w_slot, hid, spare_xT, spare_hT
        heads(nc, sem, s)
        mix_out(nc, sem, s)
        route(nc, sem, s)
        experts(nc, sem, s)


def low_half(nc, dve, t, hi_ready, hi, lo, ps, ready):
    b = t % 2
    dve.wait_ge(hi_ready, t + 1)
    cols = slice(t * P, (t + 1) * P)
    dve.tensor_tensor(lo[:, :, cols].rearrange("p (a c) q -> p a c q", a=2),
                      ps[:, 2 * b:2 * b + 2, :].rearrange("p a (c q) -> p a c q", q=P),
                      hi[:, :, cols].bitcast(F32).rearrange("p (a c) q -> p a c q", a=2),
                      ALU.subtract).then_inc(ready, 1)


def product_T(pe, ps, bank, w_hi, w_lo, xT_hi, xT_lo):
    for half in range(2):
        cols = slice(half * 512, (half + 1) * 512)
        for c in range(KC):
            pe.matmul(ps[:, bank + half, :], w_hi[:, c, :], xT_hi[:, c, cols], start=(c == 0), stop=False)
            pe.matmul(ps[:, bank + half, :], w_hi[:, c, :], xT_lo[:, c, cols], start=False, stop=False)
            ins = pe.matmul(ps[:, bank + half, :], w_lo[:, c, :], xT_hi[:, c, cols], start=False,
                            stop=(c == KC - 1))
    return ins


def heads(nc, sem, s):
    ps = s.ps
    b_hi_ready = sem("b_hi_ready")
    b_lo_ready = sem("b_lo_ready")
    q_hi_ready = sem("q_hi_ready")
    q_lo_ready = sem("q_lo_ready")
    b_multiplied = sem("b_multiplied")
    bz_ready = sem("bz_ready")
    projected = sem("projected")
    qk_squared = sem("qk_squared")
    ss_ready = sem("ss_ready")
    qk_rstd_ready = sem("qk_rstd_ready")
    qk_read = sem("qk_read")
    v_copied = sem("v_copied")
    scaled_twice = sem("scaled_twice")
    rotated = sem("rotated")
    turned = sem("turned")
    stack_hi = sem("stack_hi")
    stack_ready = sem("stack_ready")
    scores = [sem(f"scores{m}") for m in range(2)]
    max_ready = [sem(f"max_ready{m}") for m in range(2)]
    exp_done = [sem(f"exp_done{m}") for m in range(2)]
    mixed = sem("mixed")
    maps_turned = sem("maps_turned")
    mapsT_copied = sem("mapsT_copied")
    pv_done = sem("pv_done")
    o_squared = sem("o_squared")
    o_rstd_ready = sem("o_rstd_ready")
    o_scaled = sem("o_scaled")
    o_turned = sem("o_turned")
    oT_copied = sem("oT_copied")
    dve_steps = sem("dve_steps_heads")
    pool_steps = sem("pool_steps_heads")
    act_steps = sem("act_steps_heads")

    def bank_cols(b, n):
        return ps[:, b:b + 2, :].rearrange("p a n -> p (a n)")[:, 0:n]

    def score_cols(m, n):
        return bank_cols(2 + 2 * m, n)

    with nc.Block() as block:
        @block.sync
        def _(sp):
            with sp.Fori(0, HEADS - 1) as h:
                sp.wait_ge(q_lo_ready, h + 1)
                sp.wait_ge(b_lo_ready, h + 1)
                s.load_head(sp, h + 1)

        @block.scalar
        def _(act):
            own = Order(act, act_steps)
            with act.Fori(0, HEADS) as h:
                own.enter(h, NT)
                act.wait_ge(s.b_in, h * 16 + 16)
                act.wait_ge(b_multiplied, h + 1)
                act.copy(s.b_hi[:], s.b_raw[:]).then_inc(b_hi_ready, 1)
                act.wait_ge(s.q_in, h * 48 + 48)
                act.wait_ge(projected, h * NT + 1)
                act.copy(s.q_hi[:], s.q_raw[:].rearrange("p c j n -> p c (j n)")).then_inc(q_hi_ready, 1)
                for i in range(NT + 1):
                    if i < NT:
                        b = i % 2
                        act.wait_ge(projected, h * NT + (i + 2))
                        act.wait_ge(ss_ready, h * NT + (i + 1))
                        act.activation(s.qk_sq[:], ps[:, b, 0:256].rearrange("p (g d) -> p g d", g=4),
                                       ACT.Square, scale=DK ** -0.5).then_inc(qk_squared, 1)
                        act.copy(s.v_sb[:, i, :], ps[:, b, 256:384]).then_inc(v_copied, 1)
                    if i >= 1:
                        b, cols = (i - 1) % 2, slice((i - 1) * P, i * P)
                        act.wait_ge(turned, h * NT + i)
                        act.copy(s.q_stack[:, :, cols], ps[:, 6 + b, 0:256].rearrange("p (m q) -> p m q", m=2)).then_inc(stack_hi, 1)
                        act.copy(s.k_hi[:, :, cols], ps[:, 6 + b, 256:512].rearrange("p (m q) -> p m q", m=2)).then_inc(stack_hi, 1)
                for step in range(NT + 4):
                    t = step - 2
                    if 0 <= t < NT:
                        act.wait_ge(maps_turned, h * NT + (t + 1))
                        if t >= 2:
                            act.wait_ge(pv_done, h * NT + (t - 1))
                        act.copy(s.mapsT[t % 2][:, 0:t + 1, :], bank_cols(6, (t + 1) * P).rearrange("p (k q) -> p k q", q=P)).then_inc(mapsT_copied, 1)
                    if step < NT:
                        n = (step + 1) * P
                        for m in range(2):
                            act.wait_ge(max_ready[m], h * NT + (step + 1))
                            if step >= 2 and m == 0:
                                act.wait_ge(maps_turned, h * NT + (step - 1))
                            act.activation(s.probs[step % 2][:, m, 0:n], score_cols(m, n), ACT.Exp,
                                           bias=s.neg_max[:, step % 2, m:m + 1],
                                           accum_out=s.sums[:, step, m:m + 1]).then_inc(exp_done[m], 1)
                    t = step - 3
                    if 0 <= t < NT:
                        act.wait_ge(pv_done, h * NT + (t + 1))
                        if t >= 1:
                            own.wait(t)
                        own.mark(act.activation(s.o_sq[:], ps[:, 0, 0:DV], ACT.Square, scale=s.inv_sums[:, t, 0:1],
                                                accum_out=s.o_ss[:, t % 2:t % 2 + 1]))
                        own.wait(t + 1)
                        act.sem_inc(o_squared, 1)
                    t = step - 4
                    if 0 <= t < NT:
                        act.wait_ge(o_turned, h * NT + (t + 1))
                        act.activation(s.mixT[:, bass.ds(h, 1), t * P:(t + 1) * P].rearrange("p a q -> p (a q)"),
                                       ps[:, 1, 0:P], ACT.Identity, scale=s.sub_gain[:]).then_inc(oT_copied, 1)
                own.leave(HEADS)

        @block.gpsimd
        def _(pool):
            own = Order(pool, pool_steps)
            with pool.Fori(0, HEADS) as h:
                own.enter(h, 2 + NT * 4 + NT)
                pool.wait_ge(b_hi_ready, h + 1)
                pool.tensor_tensor(s.b_lo[:], s.b_raw[:], s.b_hi[:].bitcast(F32), ALU.subtract).then_inc(b_lo_ready, 1)
                pool.wait_ge(q_hi_ready, h + 1)
                pool.tensor_tensor(s.q_lo[:], s.q_raw[:].rearrange("p c j n -> p c (j n)"), s.q_hi[:].bitcast(F32),
                                   ALU.subtract).then_inc(q_lo_ready, 1)
                pool.wait_ge(bz_ready, h + 1)
                own.then(pool.tensor_tensor(s.bz_sq[:], s.bz[:], s.bz[:], ALU.mult))
                own.then(pool.tensor_tensor(s.conv_sq[:], s.conv_sq[:], s.bz_sq[:], ALU.add))
                for i in range(NT):
                    b = i % 2
                    pool.wait_ge(ss_ready, h * NT + (i + 2))
                    own.then(pool.tensor_tensor(s.qk_rstd[:, b, :], s.qk_ss[:, b, :], s.eps_qk[:, 0:4], ALU.add))
                    pool.tensor_tensor(s.qk_rstd[:, b, :], s.qk_rstd[:, b, :], s.neg_half[:, 0:4], ALU.pow).then_inc(qk_rstd_ready, 1)
                    pool.wait_ge(scaled_twice, h * NT + (i + 1))
                    twice = s.qk_twice[b]
                    half = ROT // 2
                    own.mark(pool.tensor_tensor(s.rot_a[:], twice[:, :, 0, 0:ROT],
                                                s.cos2[:, i:i + 1, :].to_broadcast([P, 4, ROT]), ALU.mult))
                    own.mark(pool.tensor_tensor(s.rot_b[:, :, 0:half], twice[:, :, 0, half:ROT],
                                                s.sin2[:, i:i + 1, 0:half].to_broadcast([P, 4, half]), ALU.mult))
                    own.then(pool.tensor_tensor(s.rot_b[:, :, half:ROT], twice[:, :, 0, 0:half],
                                                s.sin2[:, i:i + 1, half:ROT].to_broadcast([P, 4, half]), ALU.mult))
                    pool.tensor_tensor(twice[:, :, :, 0:ROT], s.rot_a[:].unsqueeze(2).to_broadcast([P, 4, 2, ROT]),
                                       s.rot_b[:].unsqueeze(2).to_broadcast([P, 4, 2, ROT]), ALU.add).then_inc(rotated, 1)
                    pool.wait_ge(rotated, h * NT + (i + 1))
                for t in range(NT):
                    c = slice(t % 2, t % 2 + 1)
                    pool.wait_ge(o_squared, h * NT + (t + 1))
                    own.then(pool.tensor_tensor(s.o_rstd[:, c], s.o_ss[:, c], s.eps_o[:], ALU.add))
                    pool.tensor_tensor(s.o_rstd[:, c], s.o_rstd[:, c], s.neg_half[:, 0:1], ALU.pow).then_inc(o_rstd_ready, 1)
                own.leave(HEADS)

        @block.vector
        def _(dve):
            own = Order(dve, dve_steps)
            dve.sem_inc(ss_ready, 1)
            dve.sem_inc(o_scaled, 1)
            with dve.Fori(0, HEADS) as h:
                own.enter(h, 2 + NT + 2 * NT)
                z = s.mixT[:, bass.ds(h + HEADS, 1), :].rearrange("p c t -> p (c t)")
                own.mark(dve.tensor_copy(s.g_taps[:], s.conv_taps[:, bass.ds(h, 1), :].rearrange("p m j -> p (m j)")))
                dve.wait_ge(b_multiplied, h + 2)
                dve.tensor_tensor(s.bz[:].rearrange("p (a n) -> p a n", a=2), ps[:, 0:2, :],
                                  z.rearrange("p (a n) -> p a n", a=2), ALU.mult).then_inc(bz_ready, 1)
                dve.wait_ge(bz_ready, h + 1)
                own.wait(1)
                own.mark(dve.tensor_scalar(z, s.bz[:], s.g_taps[:, 3:4], None, ALU.mult))
                for i in range(NT + 1):
                    if i < NT:
                        b = i % 2
                        dve.wait_ge(qk_squared, h * NT + (i + 1))
                        dve.reduce_sum(s.qk_ss[:, b, :], s.qk_sq[:], axis=AX.X).then_inc(ss_ready, 1)
                        dve.wait_ge(qk_rstd_ready, h * NT + (i + 1))
                        dve.wait_ge(v_copied, h * NT + (i + 1))
                        dve.tensor_tensor(s.qk_scaled[0][:], ps[:, b, 0:256].rearrange("p (g d) -> p g d", g=4),
                                          s.qk_rstd[:, b, :].unsqueeze(2).to_broadcast([P, 4, DK]), ALU.mult).then_inc(qk_read, 1)
                        dve.wait_ge(qk_read, h * NT + (i + 1))
                        if i >= 2:
                            dve.wait_ge(turned, h * NT + (i - 1))
                        own.mark(dve.tensor_tensor(s.qk_twice[b][:], s.qk_scaled[0][:].unsqueeze(2).to_broadcast([P, 4, 2, DK]),
                                                   s.qk_gain[:].rearrange("p a m d -> p (a m) d").unsqueeze(2).to_broadcast([P, 4, 2, DK]),
                                                   ALU.mult))
                        own.wait(own.n)
                        dve.sem_inc(scaled_twice, 1)
                    if i >= 1:
                        t = i - 1
                        b, cols = t % 2, slice(t * P, i * P)
                        dve.wait_ge(stack_hi, h * (2 * NT) + (2 * t + 2))
                        dve.tensor_tensor(s.q_stack[DK:, :, cols], ps[DK:, 6 + b, 0:256].rearrange("p (m q) -> p m q", m=2),
                                          s.q_stack[DK:, :, cols].bitcast(F32), ALU.subtract).then_inc(stack_ready, 1)
                        dve.tensor_tensor(s.k_lo[:, :, cols], ps[:, 6 + b, 256:512].rearrange("p (m q) -> p m q", m=2),
                                          s.k_hi[:, :, cols].bitcast(F32), ALU.subtract).then_inc(stack_ready, 1)
                for step in range(NT + 3):
                    if step < NT:
                        for m in range(2):
                            dve.wait_ge(scores[m], h * NT + (step + 1))
                            dve.tensor_reduce(s.neg_max[:, step % 2, m:m + 1], score_cols(m, (step + 1) * P), axis=AX.X,
                                              op=ALU.max, negate=True).then_inc(max_ready[m], 1)
                    t = step - 1
                    if 0 <= t < NT:
                        n = (t + 1) * P
                        for m in range(2):
                            dve.wait_ge(exp_done[m], h * NT + (t + 2))
                        own.then(dve.reciprocal(s.inv_sums[:, t, :], s.sums[:, t, :]))
                        own.then(dve.tensor_scalar(s.ratio[:, 0:1], s.inv_sums[:, t, 1:2], s.sums[:, t, 0:1], s.neg_lam[:],
                                                   ALU.mult, ALU.mult))
                        dve.scalar_tensor_tensor(s.probs[t % 2][:, 0, 0:n], s.probs[t % 2][:, 1, 0:n], s.ratio[:, 0:1],
                                                 s.probs[t % 2][:, 0, 0:n], ALU.mult, ALU.add).then_inc(mixed, 1)
                    t = step - 3
                    if 0 <= t < NT:
                        dve.wait_ge(o_rstd_ready, h * NT + (t + 1))
                        if t >= 2:
                            dve.wait_ge(o_turned, h * NT + (t - 1))
                        dve.tensor_scalar(s.o_sb[t % 2][:], ps[:, 0, 0:DV], s.inv_sums[:, t, 0:1], s.o_rstd[:, t % 2:t % 2 + 1],
                                          ALU.mult, ALU.mult).then_inc(o_scaled, 1)
                own.leave(HEADS)

        @block.tensor
        def _(pe):
            for primed in (b_multiplied, projected, exp_done[0], exp_done[1], oT_copied):
                pe.sem_inc(primed, 1)
            with pe.Fori(0, HEADS) as h:
                pe.wait_ge(b_lo_ready, h + 1)
                pe.wait_ge(o_scaled, h * NT + 1)
                pe.wait_ge(oT_copied, h * NT + 1)
                product_T(pe, ps, 0, s.b_hi, s.b_lo, s.xT_hi, s.xT_lo).then_inc(b_multiplied, 1)
                pe.wait_ge(q_lo_ready, h + 1)
                pe.wait_ge(bz_ready, h + 1)
                for i in range(NT + 1):
                    if i < NT:
                        cols = slice(i * P, (i + 1) * P)
                        if i >= 2:
                            pe.wait_ge(qk_read, h * NT + (i - 1))
                            pe.wait_ge(v_copied, h * NT + (i - 1))
                        o = ps[:, i % 2, 0:3 * P]
                        for c in range(KC):
                            pe.matmul(o, s.xT_hi[:, c, cols], s.q_hi[:, c, :], start=(c == 0), stop=False)
                            pe.matmul(o, s.xT_hi[:, c, cols], s.q_lo[:, c, :], start=False, stop=False)
                            ins = pe.matmul(o, s.xT_lo[:, c, cols], s.q_hi[:, c, :], start=False, stop=(c == KC - 1))
                        ins.then_inc(projected, 1)
                    if i >= 1:
                        t = i - 1
                        pe.wait_ge(rotated, h * NT + i)
                        if t >= 2:
                            pe.wait_ge(stack_ready, h * (2 * NT) + 2 * (t - 1))
                        for g in range(4):
                            ins = pe.transpose(ps[:, 6 + t % 2, g * P:(g + 1) * P],
                                               s.qk_twice[t % 2][:, g, :, :].rearrange("p e d -> p (e d)"), s.ident[:])
                        ins.then_inc(turned, 1)
                for step in range(NT + 4):
                    if step < NT:
                        if step == 0:
                            pe.wait_ge(stack_ready, h * (2 * NT) + 2 * NT)
                        n = (step + 1) * P
                        for m in range(2):
                            pe.wait_ge(exp_done[m], h * NT + (step + 1))
                            q = s.q_stack[:, m, step * P:n]
                            for k0 in range(0, n, 512):
                                k1 = min(k0 + 512, n)
                                o = score_cols(m, 1024)[:, k0:k1]
                                pe.matmul(o, q, s.k_hi[:, m, k0:k1], start=True, stop=False)
                                if k1 == n:
                                    pe.matmul(o[:, k1 - k0 - P:], s.ident_b[:], s.causal_b[:], start=False,
                                              stop=False, skip_group_check=True)
                                ins = pe.matmul(o, q, s.k_lo[:, m, k0:k1], start=False, stop=True)
                            ins.then_inc(scores[m], 1)
                    t = step - 2
                    if 0 <= t < NT:
                        pe.wait_ge(mixed, h * NT + (t + 1))
                        if t >= 1:
                            pe.wait_ge(mapsT_copied, h * NT + t)
                        for k in range(t + 1):
                            ins = pe.transpose(ps[:, 6 + k // 4, (k % 4) * P:(k % 4 + 1) * P],
                                               s.probs[t % 2][:, 0, k * P:(k + 1) * P], s.ident[:])
                        ins.then_inc(maps_turned, 1)
                    t = step - 3
                    if 0 <= t < NT:
                        pe.wait_ge(mapsT_copied, h * NT + (t + 1))
                        if t == 0:
                            pe.wait_ge(v_copied, h * NT + NT)
                        pe.wait_ge(o_scaled, h * NT + (t + 1))
                        for k in range(t + 1):
                            ins = pe.matmul(ps[:, 0, 0:DV], s.mapsT[t % 2][:, k, :], s.v_sb[:, k, :],
                                            start=(k == 0), stop=(k == t))
                        ins.then_inc(pv_done, 1)
                    t = step - 4
                    if 0 <= t < NT:
                        pe.wait_ge(o_scaled, h * NT + (t + 2))
                        pe.wait_ge(oT_copied, h * NT + (t + 1))
                        pe.transpose(ps[:, 1, 0:P], s.o_sb[t % 2][:], s.ident[:]).then_inc(o_turned, 1)


def mix_out(nc, sem, s):
    ps = s.ps
    wo_in = [sem(f"wo_in{b}") for b in range(2)]
    xa_in = [sem(f"xa_in{b}") for b in range(2)]
    gain2_in = sem("gain2_in")
    route_in = sem("route_in")
    wo_hi_ready = sem("wo_hi_ready")
    wo_lo_ready = sem("wo_lo_ready")
    conv_summed = sem("conv_summed")
    conv_mean = sem("conv_mean")
    conv_rstd = sem("conv_rstd")
    m_hi_ready = sem("m_hi_ready")
    m_lo_ready = sem("m_lo_ready")
    product_done = sem("product_done")
    part_added = sem("part_added")
    h_ready = sem("h_ready")
    h_squared = sem("h_squared")
    h_rstd_ready = sem("h_rstd_ready")
    hn_ready = sem("hn_ready")
    hn_turned = sem("hn_turned")
    hnT_copied = sem("hnT_copied")
    routed = sem("routed")
    logits_copied = sem("logits_copied")
    h_stored = sem("h_stored")
    hn_stored = sem("hn_stored")
    stored = sem("stored")
    pool_steps = sem("pool_steps_mix")
    wo_k = s.w_out[0].rearrange("(k p) n -> p k n", p=P)

    def turns(eng, turn):
        with eng.Fori(0, (NT - 2) // 2) as j:
            for b in range(2):
                turn(j * 2 + b, j + b, b, True)
        turn(NT - 2, (NT - 1) // 2, 0, True)
        turn(NT - 1, None, 1, False)

    with nc.Block() as block:
        @block.sync
        def _(sp):
            sp.sem_inc(stored, 1)
            for k in range(KC):
                if k >= 2:
                    sp.wait_ge(wo_lo_ready, k - 1)
                sp.dma_start(s.wo_raw[k % 2][:], wo_k[:, k, :]).then_inc(wo_in[k % 2], 16)
                if k < 2:
                    sp.dma_start(s.x_again[k][:], s.x_rows[k * P:(k + 1) * P, :]).then_inc(xa_in[k], 16)
                if k == 2:
                    sp.dma_start(s.gain2[:], s.ffn_norm_gain[0:1, :].to_broadcast([P, D])).then_inc(gain2_in, 16)

            def turn(t, half, b, more):
                sp.wait_ge(h_ready, t + 1)
                sp.dma_start(s.out_rows[bass.ds(t * P, P), :], s.h_sb[b][:]).then_inc(h_stored, 16)
                sp.wait_ge(hn_ready, t + 1)
                sp.dma_start(s.xn2_rows[bass.ds(t * P, P), :], s.hn[b][:].rearrange("p c q -> p (c q)")).then_inc(hn_stored, 16)
                if not isinstance(t, int):
                    sp.dma_start(s.x_again[b][:], s.x_rows[bass.ds(t * P + 2 * P, P), :]).then_inc(xa_in[b], 16)
                sp.wait_ge(h_stored, t * 16 + 16)
                sp.wait_ge(hn_stored, t * 16 + 16)
                sp.sem_inc(stored, 1)

            turns(sp, turn)

        @block.gpsimd
        def _(pool):
            own = Order(pool, pool_steps)
            with nc.allow_non_contiguous_dma(reason="the routers' narrow weights"):
                pool.dma_start(s.w_route[:, :, 0:GROUPS], s.w_group_router[0].rearrange("(p c) g -> p c g", c=KC)).then_inc(route_in, 16)
                for g in range(GROUPS):
                    pool.dma_start(s.w_route[:, :, GROUPS + g * PER_GROUP:GROUPS + (g + 1) * PER_GROUP],
                                   s.w_expert_router[0, g].rearrange("(p c) e -> p c e", c=KC)).then_inc(route_in, 16)
            pool.wait_ge(conv_mean, 1)
            pool.tensor_tensor(s.rstd_c[:], s.rstd_c[:], s.neg_half[:], ALU.pow).then_inc(conv_rstd, 1)
            with pool.Fori(0, NT // 2) as j:
                own.enter(j, 2)
                for b in range(2):
                    pool.wait_ge(h_squared, j * 2 + (b + 2))
                    own.then(pool.tensor_tensor(s.h_rstd[:, b:b + 1], s.h_ss[:, b:b + 1], s.eps_qk[:, 0:1], ALU.add))
                    pool.tensor_tensor(s.h_rstd[:, b:b + 1], s.h_rstd[:, b:b + 1], s.neg_half[:, 0:1], ALU.pow).then_inc(h_rstd_ready, 1)
                own.leave(NT // 2)

        @block.scalar
        def _(act):
            def round_mix(t, b):
                act.copy(s.m_hi[b][:], s.mixT[:, :, bass.ds(t * P, P)]).then_inc(m_hi_ready, 1)

            round_mix(0, 0)
            for k in range(KC):
                act.wait_ge(wo_in[k % 2], 16 * (k // 2 + 1))
                act.copy(s.wo_hi[:, k, :], s.wo_raw[k % 2][:]).then_inc(wo_hi_ready, 1)
            round_mix(1, 1)

            def turn(t, half, b, more):
                if not isinstance(t, int):
                    act.wait_ge(product_done, t * 2 + 2)
                    round_mix(t + 2, b)
                act.wait_ge(h_ready, t + 1)
                act.wait_ge(h_squared, t + 1)
                act.activation(s.h_sq[:], s.h_sb[b][:], ACT.Square, scale=D ** -0.5,
                               accum_out=s.h_ss[:, b:b + 1]).then_inc(h_squared, 1)
                act.wait_ge(hn_turned, t + 1)
                act.wait_ge(routed, t + 1)
                act.copy(s.hnT[:].rearrange("p (a c) q -> p a (c q)", a=2), ps[:, 4:6, :]).then_inc(hnT_copied, 1)
                act.wait_ge(routed, t + 2)
                act.copy(s.logits[:, bass.ds(t, 1), :].rearrange("p a g -> p (a g)"), ps[:, 6, 0:GROUPS + E]).then_inc(logits_copied, 1)

            turns(act, turn)

        @block.vector
        def _(dve):
            def low_mix(t, b):
                dve.wait_ge(m_hi_ready, t + 1)
                dve.tensor_tensor(s.m_lo[b][:], s.mixT[:, :, bass.ds(t * P, P)], s.m_hi[b][:].bitcast(F32),
                                  ALU.subtract).then_inc(m_lo_ready, 1)

            def add_parts(t, uses, b):
                dve.wait_ge(xa_in[b], uses * 16 + 16)
                dve.wait_ge(product_done, t * 2 + 1)
                banks = lambda n: ps[:, n:n + 2, :].rearrange("p a n -> p (a n)")
                dve.tensor_tensor(s.h_sb[b][:], banks(0), s.x_again[b][:], ALU.add).then_inc(part_added, 1)
                dve.wait_ge(part_added, t + 1)
                dve.wait_ge(product_done, t * 2 + 2)
                dve.scalar_tensor_tensor(s.h_sb[b][:], banks(2), s.rstd_c[:, bass.ds(t, 1)], s.h_sb[b][:],
                                         ALU.mult, ALU.add).then_inc(h_ready, 1)

            dve.sem_inc(h_squared, 1)
            low_mix(0, 0)
            for k in range(KC):
                dve.wait_ge(wo_hi_ready, k + 1)
                dve.tensor_tensor(s.wo_lo[:, k, :], s.wo_raw[k % 2][:], s.wo_hi[:, k, :].bitcast(F32),
                                  ALU.subtract).then_inc(wo_lo_ready, 1)
            low_mix(1, 1)
            dve.wait_ge(conv_summed, 1)
            dve.tensor_scalar(s.rstd_c[:], ps[:, 7, 0:NT], 1.0 / CONV, EPS, ALU.mult, ALU.add).then_inc(conv_mean, 1)
            dve.wait_ge(conv_rstd, 1)
            dve.wait_ge(gain2_in, 16)
            add_parts(0, 0, 0)

            def turn(t, half, b, more):
                if not isinstance(t, int):
                    low_mix(t + 2, b)
                dve.wait_ge(h_rstd_ready, t + 1)
                rows = lambda a: a.rearrange("p (q c) -> p q c", c=KC)
                dve.scalar_tensor_tensor(s.hn[b][:].rearrange("p c q -> p q c"), rows(s.h_sb[b][:]), s.h_rstd[:, b:b + 1],
                                         rows(s.gain2[:]), ALU.mult, ALU.mult).then_inc(hn_ready, 1)
                if more:
                    dve.wait_ge(stored, t + 1)
                    add_parts(t + 1, half, 1 - b)

            turns(dve, turn)

        @block.tensor
        def _(pe):
            def part(t, b, n):
                for k in range(4 * n, 4 * n + 4):
                    first, last = k == 4 * n, k == 4 * n + 3
                    if isinstance(t, int) and t == 0:
                        pe.wait_ge(wo_lo_ready, k + 1)
                    for half in range(2):
                        o, cols = ps[:, 2 * n + half, :], slice(half * 512, (half + 1) * 512)
                        pe.matmul(o, s.m_hi[b][:, k, :], s.wo_hi[:, k, cols], start=first, stop=False)
                        pe.matmul(o, s.m_hi[b][:, k, :], s.wo_lo[:, k, cols], start=False, stop=False)
                        ins = pe.matmul(o, s.m_lo[b][:, k, :], s.wo_hi[:, k, cols], start=False, stop=last)
                ins.then_inc(product_done, 1)

            pe.sem_inc(hnT_copied, 1)
            pe.sem_inc(logits_copied, 1)
            pe.sem_inc(routed, 1)
            for t in range(NT):
                ins = pe.matmul(ps[:, 7, t:t + 1], s.conv_sq[:, t * P:(t + 1) * P], s.ones_col[:], start=True, stop=True)
            ins.then_inc(conv_summed, 1)
            pe.wait_ge(m_lo_ready, 1)
            part(0, 0, 0)
            part(0, 0, 1)
            pe.wait_ge(route_in, 16 * (1 + GROUPS))

            def turn(t, half, b, more):
                if more:
                    pe.wait_ge(m_lo_ready, t + 2)
                    pe.wait_ge(part_added, t + 1)
                    part(t + 1, 1 - b, 0)
                pe.wait_ge(hn_ready, t + 1)
                pe.wait_ge(hnT_copied, t + 1)
                for c in range(KC):
                    ins = pe.transpose(ps[:, 4 + c // 4, (c % 4) * P:(c % 4 + 1) * P], s.hn[b][:, c, :], s.ident[:])
                ins.then_inc(hn_turned, 1)
                if more:
                    pe.wait_ge(h_ready, t + 1)
                    part(t + 1, 1 - b, 1)
                pe.wait_ge(hnT_copied, t + 2)
                pe.wait_ge(logits_copied, t + 1)
                for c in range(KC):
                    ins = pe.matmul(ps[:, 6, 0:GROUPS + E], s.hnT[:, c, :], s.w_route[:, c, :], start=(c == 0), stop=(c == KC - 1))
                ins.then_inc(routed, 1)

            turns(pe, turn)




def route(nc, sem, s):
    ps = s.ps
    iotas = sem("iotas")
    shifted = sem("shifted")
    group_exp = sem("group_exp")
    top_diff = sem("top_diff")
    top_exp = sem("top_exp")
    chosen = sem("chosen")
    counted = sem("counted")
    table_parts = sem("table_parts")
    table_summed = sem("table_summed")
    dve_steps = sem("dve_steps_route")
    L = s.logits
    room = Shared()
    room.kb = 104.0

    def tile(name, shape, dtype=F32):
        n = 1
        for d in shape[1:]:
            n *= d
        t = s.at(name, room.kb, shape, dtype)
        room.kb += -(-n * (2 if dtype == BF16 else 4) // 32) / 32
        return t

    iota_e = tile("iota_e", [P, E])
    iota_r = tile("iota_r", [P, P])
    iota_b = tile("iota_b", [P, BLOCKS])
    full = tile("full", [P, NT - 1])
    tok = tile("tok", [P, NT])
    gl = tile("gl", [P, NT, GROUPS])
    gtmp = tile("gtmp", [P, NT, GROUPS])
    gmask = tile("gmask", [P, NT, GROUPS])
    stat = [tile(f"stat{j}", [P, NT]) for j in range(8)]
    gate = tile("gate", [P, NT])
    el = tile("el", [P, NT, E])
    tmp = tile("tmp", [P, NT, E])
    hot = [tile(f"hot{k}", [P, NT, E]) for k in range(TOP_K)]
    mask = tile("mask", [P, NT, E], BF16)
    pos = tile("pos", [P, NT, E])
    weight = tile("weight", [P, TOP_K, NT])
    cnt = tile("cnt", [P, E])
    over = tile("over", [P, E, NT - 1])
    extra = tile("extra", [P, E])
    ends = tile("ends", [P, E])
    starts = tile("starts", [P, E])
    ones_e = tile("ones_e", [P, E])
    passed = tile("passed", [P, SPARE, E])
    spare_f = tile("spare_f", [P, SPARE])
    slot = tile("slot", [P, TOP_K, NT])
    own_e = tile("own_e", [P, TOP_K, NT])
    first = tile("first", [P, TOP_K, NT])
    nth = tile("nth", [P, TOP_K, NT])
    beyond = tile("beyond", [P, TOP_K * NT, NT - 1])
    later = tile("later", [P, TOP_K, NT])
    in_slot = tile("in_slot", [P, TOP_K * NT, P])
    in_block = tile("in_block", [P, TOP_K * NT, BLOCKS])
    entry = tile("entry", [P, TOP_K * NT, 2, BLOCKS])
    table_f = tile("table_f", [P, 2, BLOCKS])
    assert room.kb <= 150

    with nc.Block() as block:
        @block.sync
        def _(sp):
            for e in range(2):
                for q in range(4):
                    s.load_gate_up(sp, e, e, q)
            for e in range(2):
                for q in range(2):
                    s.load_down(sp, e, e, q)

        @block.gpsimd
        def _(pool):
            def iota(out, pattern, base, per_partition=0):
                pool.iota(out, pattern=pattern, base=base, channel_multiplier=per_partition,
                          allow_small_or_imprecise_dtypes=True).then_inc(iotas, 1)

            iota(iota_e[:], [[1, E]], 0)
            iota(iota_r[:], [[1, P]], 0)
            iota(iota_b[:], [[1, BLOCKS]], 0)
            iota(full[:], [[P, NT - 1]], P)
            iota(tok[:], [[P, NT]], -NO_TOKEN, 1)
            pool.memset(ones_e[:], 1.0).then_inc(iotas, 1)
            for b in range(2):
                pool.memset(s.rows[b][:], 0.0).then_inc(iotas, 1)

        @block.scalar
        def _(act):
            act.wait_ge(shifted, 1)
            act.activation(gl[:], gl[:], ACT.Exp).then_inc(group_exp, 1)
            act.wait_ge(top_diff, 1)
            act.activation(stat[5][:], stat[5][:], ACT.Exp).then_inc(top_exp, 1)

        @block.vector
        def _(dve):
            own = Order(dve, dve_steps)
            do = own.then
            wide = lambda a, n: a.unsqueeze(2).to_broadcast([P, NT, n])
            row = lambda a, n, m: a.unsqueeze(1).to_broadcast([P, n, m])
            mul, add, sub, ge, gt, eq = ALU.mult, ALU.add, ALU.subtract, ALU.is_ge, ALU.is_gt, ALU.is_equal

            def lowest(out, values, top, n, scratch, low):
                do(dve.tensor_tensor(scratch, values, wide(top, n), ge))
                do(dve.scalar_tensor_tensor(scratch, scratch, -100.0, row(iota_e[:, 0:n], NT, n), mul, add))
                do(dve.tensor_reduce(low, scratch, axis=AX.X, op=ALU.min))
                do(dve.tensor_tensor(out, scratch, wide(low, n), eq))

            dve.wait_ge(iotas, 8)
            gmax, low, v1, gsum, v2, diff, total = (a[:] for a in stat[:7])
            gates = L[:, :, 0:GROUPS]
            do(dve.tensor_reduce(gmax, gates, axis=AX.X, op=ALU.max))
            dve.tensor_tensor(gl[:], gates, wide(gmax, GROUPS), sub).then_inc(shifted, 1)
            lowest(gmask[:], gates, gmax, GROUPS, gtmp[:], low)
            do(dve.tensor_scalar(gtmp[:], gmask[:], -MASKED, MASKED, mul, add))
            by_group = lambda a: a.rearrange("p t (g e) -> p t g e", g=GROUPS)
            of_group = lambda a: a.unsqueeze(3).to_broadcast([P, NT, GROUPS, PER_GROUP])
            do(dve.tensor_tensor(by_group(el[:]), by_group(L[:, :, GROUPS:]), of_group(gmask[:]), mul))
            do(dve.tensor_tensor(by_group(el[:]), by_group(el[:]), of_group(gtmp[:]), add))
            do(dve.tensor_reduce(v1, el[:], axis=AX.X, op=ALU.max))
            lowest(hot[0][:], el[:], v1, E, tmp[:], low)
            do(dve.scalar_tensor_tensor(el[:], hot[0][:], 2 * MASKED, el[:], mul, add))
            do(dve.tensor_reduce(v2, el[:], axis=AX.X, op=ALU.max))
            dve.tensor_tensor(diff, v2, v1, sub).then_inc(top_diff, 1)
            lowest(hot[1][:], el[:], v2, E, tmp[:], low)
            dve.tensor_tensor(mask[:], hot[0][:], hot[1][:], add).then_inc(chosen, 1)
            dve.wait_ge(group_exp, 1)
            do(dve.reduce_sum(gsum, gl[:], axis=AX.X))
            dve.wait_ge(top_exp, 1)
            do(dve.tensor_scalar(total, diff, 1.0, None, add))
            do(dve.tensor_tensor(total, total, gsum, mul))
            do(dve.reciprocal(weight[:, 0, :], total))
            do(dve.tensor_tensor(weight[:, 1, :], weight[:, 0, :], diff, mul))
            for k in range(TOP_K):
                do(dve.tensor_tensor(tmp[:], hot[k][:], row(iota_e[:], NT, E), mul))
                do(dve.reduce_sum(own_e[:, k, :], tmp[:], axis=AX.X))
            dve.wait_ge(counted, 1)
            do(dve.tensor_copy(cnt[:], ps[:, 1, 0:E]))
            do(dve.tensor_tensor(over[:], cnt[:].unsqueeze(2).to_broadcast([P, E, NT - 1]), row(full[:], E, NT - 1), gt))
            do(dve.reduce_sum(extra[:], over[:], axis=AX.X))
            do(dve.tensor_tensor_scan(ends[:], ones_e[:], extra[:], 0.0, mul, add))
            do(dve.tensor_tensor(starts[:], ends[:], extra[:], sub))
            do(dve.tensor_copy(s.spare_n[:], ends[:, E - 1:E]))
            do(dve.tensor_tensor(passed[:], row(ends[:], SPARE, E), iota_b[:, 0:SPARE].unsqueeze(2).to_broadcast([P, SPARE, E]),
                                 ALU.is_le))
            do(dve.reduce_sum(spare_f[:], passed[:], axis=AX.X))
            do(dve.tensor_scalar(s.spare_e[:], spare_f[:], E - 1.0, None, ALU.min))
            for k in range(TOP_K):
                do(dve.tensor_tensor(pos[:], hot[k][:], ps[:, 0, 0:NT * E].rearrange("p (t e) -> p t e", e=E), mul))
                do(dve.reduce_sum(slot[:, k, :], pos[:], axis=AX.X))
                do(dve.tensor_tensor(tmp[:], hot[k][:], row(starts[:], NT, E), mul))
                do(dve.reduce_sum(first[:, k, :], tmp[:], axis=AX.X))
            flat = lambda a: a.rearrange("p k t -> p (k t)")
            do(dve.tensor_tensor(beyond[:], flat(slot[:]).unsqueeze(2).to_broadcast([P, TOP_K * NT, NT - 1]),
                                 row(full[:], TOP_K * NT, NT - 1), ge))
            do(dve.reduce_sum(flat(nth[:]), beyond[:], axis=AX.X))
            do(dve.scalar_tensor_tensor(slot[:], nth[:], -float(P), slot[:], mul, add))
            do(dve.tensor_scalar(later[:], nth[:], 1.0, None, ALU.min))
            do(dve.tensor_tensor(first[:], first[:], nth[:], add))
            do(dve.tensor_scalar(first[:], first[:], E - 1.0, None, add))
            do(dve.tensor_tensor(first[:], first[:], own_e[:], sub))
            do(dve.tensor_tensor(first[:], first[:], later[:], mul))
            do(dve.tensor_tensor(own_e[:], own_e[:], first[:], add))
            every = lambda a, n: a.unsqueeze(2).to_broadcast([P, TOP_K * NT, n])
            do(dve.tensor_tensor(in_slot[:], every(flat(slot[:]), P), row(iota_r[:], TOP_K * NT, P), eq))
            do(dve.tensor_tensor(in_block[:], every(flat(own_e[:]), BLOCKS), row(iota_b[:], TOP_K * NT, BLOCKS), eq))
            for k in range(TOP_K):
                part = slice(k * NT, (k + 1) * NT)
                do(dve.tensor_tensor(entry[:, part, 0, :], in_block[:, part, :], wide(tok[:], BLOCKS), mul))
            do(dve.tensor_tensor(entry[:, :, 1, :], in_block[:], every(flat(weight[:]), BLOCKS), mul))
            dve.sem_inc(table_parts, 1)
            dve.wait_ge(table_summed, 1)
            do(dve.tensor_copy(table_f[:], ps[:, 2, 0:2 * BLOCKS].rearrange("p (a b) -> p a b", a=2)))
            do(dve.tensor_scalar(s.table[:, :, 0], table_f[:, 0, :], float(NO_TOKEN), None, add))
            do(dve.tensor_copy(s.table[:, :, 1].bitcast(F32), table_f[:, 1, :]))

        @block.tensor
        def _(pe):
            pe.wait_ge(chosen, 1)
            for t in range(NT):
                for b in range(t + 1):
                    pe.matmul(ps[:, 0, t * E:(t + 1) * E], s.before_b[:] if b == t else s.ones_b[:], mask[:, b, :],
                              start=(b == 0), stop=(b == t))
            for t in range(NT):
                ins = pe.matmul(ps[:, 1, 0:E], s.ones_b[:], mask[:, t, :], start=(t == 0), stop=(t == NT - 1))
            ins.then_inc(counted, 1)
            pe.wait_ge(table_parts, 1)
            n = TOP_K * NT
            for j in range(n):
                ins = pe.matmul(ps[:, 2, 0:2 * BLOCKS], in_slot[:, j, :], entry[:, j, :, :].rearrange("p a b -> p (a b)"),
                                start=(j == 0), stop=(j == n - 1))
            ins.then_inc(table_summed, 1)


def experts(nc, sem, s):
    ps = s.ps
    hi_ready = [sem(f"hi_ready{k}") for k in range(6)]
    lo_ready = [sem(f"lo_ready{k}") for k in range(6)]
    used = [sem(f"used{k}") for k in range(6)]
    rows_in = [sem(f"rows_in{b}") for b in range(2)]
    scattered = sem("scattered")
    waited = sem("waited")
    y_free = sem("y_free")
    gather_idx = sem("gather_idx")
    scatter_idx = sem("scatter_idx")
    rows_turned = sem("rows_turned")
    rT_hi_ready = sem("rT_hi_ready")
    rT_lo_ready = sem("rT_lo_ready")
    gated = sem("gated")
    silu_ready = sem("silu_ready")
    weight_ready = sem("weight_ready")
    hid_ready = sem("hid_ready")
    hid_turned = sem("hid_turned")
    hT_hi_ready = sem("hT_hi_ready")
    hT_lo_ready = sem("hT_lo_ready")
    down_done = sem("down_done")
    y_ready = [sem(f"y_ready{n}") for n in range(2)]

    def has(e):
        return not isinstance(e, int) or 0 <= e < E

    def after(eng, semaphore, e, step=1):
        if not isinstance(e, int) or e >= 0:
            eng.wait_ge(semaphore, (e + 1) * step)

    def turns(turn):
        def run(eng):
            for e in range(-2, 2):
                turn(e, e % 2, e // 2)
            with eng.Fori(0, (E - 4) // 2) as j:
                for b in range(2):
                    turn(j * 2 + (b + 2), b, j + 1)
            for e in range(E - 2, E + 2):
                turn(e, e % 2, e // 2)
        return run

    def rows_loaded(eng, e, b, h, k):
        if has(e + k):
            eng.wait_ge(rows_in[(b + k) % 2], (h + (b + k) // 2 + 1) * 16)

    def split_hi(act, e, b, h, d, k):
        if has(e + d):
            act.wait_ge(s.loaded[(b + d) % 2][k], (h + (b + d) // 2 + 1) * (32 if k < 4 else 16))
            after(act, used[k], e + (d - 1))
            act.copy(s.w_hi[k][:], s.raw[(b + d) % 2][k][:]).then_inc(hi_ready[k], 1)

    def split_lo(eng, e, b, d, k):
        if has(e + d):
            after(eng, hi_ready[k], e + d)
            eng.tensor_tensor(s.w_lo[(b + d) % 2][k][:], s.raw[(b + d) % 2][k][:], s.w_hi[k][:].bitcast(F32),
                              ALU.subtract).then_inc(lo_ready[k], 1)

    banks45 = ps[:, 4:6, :]
    as_banks = lambda a: a.rearrange("p (a c) q -> p a (c q)", a=2)

    with nc.Block() as block:
        @block.sync
        def _(sp):
            def turn(e, b, h):
                for q in range(4):
                    after(sp, used[q], e - 1)
                    s.load_gate_up(sp, e + 1, 1 - b, q)
                for q in range(2):
                    after(sp, used[4 + q], e - 2)
                    s.load_down(sp, e, b, q)

            for q in range(4):
                sp.wait_ge(used[q], 1)
                s.load_gate_up(sp, 2, 0, q)
            with sp.Fori(0, (E - 4) // 2) as j:
                for b in range(2):
                    turn(j * 2 + (b + 2), b, None)
            turn(E - 2, 0, None)
            for q in range(2):
                after(sp, used[4 + q], E - 3)
                s.load_down(sp, E - 1, 1, q)

        @block.gpsimd
        def _(pool):
            last_row = pool.to_reg(T - 1)
            pool.sem_inc(y_free, 2)

            def turn(e, b, h):
                if has(e + 2):
                    after(pool, gather_idx, e + 2)
                    after(pool, rows_turned, e)
                    pool.sem_inc(waited, 1)
                    pool.indirect_dma_start(
                        out=s.rows[b][:].rearrange("p c q -> p (c q)"), out_offset=None, in_=s.xn2_rows,
                        in_offset=bass.IndirectOffsetOnAxis(ap=s.idx_g[b][:, 0:1], axis=0),
                        bounds_check=last_row, oob_is_err=False).then_inc(rows_in[b], 16)
                if has(e - 2):
                    after(pool, scatter_idx, e - 2)
                    for n in range(2):
                        after(pool, y_ready[n], e - 2)
                    pool.sem_inc(waited, 1)
                    pool.indirect_dma_start(
                        out=s.out_rows, out_offset=bass.IndirectOffsetOnAxis(ap=s.idx_s[b][:, 0:1], axis=0),
                        in_=s.y_sb[b][:], in_offset=None, bounds_check=last_row, oob_is_err=False,
                        compute_op=ALU.add).then_inc(scattered, 16)
                split_lo(pool, e, b, -1, 5)
                if has(e - 2):
                    after(pool, scattered, e - 2, 16)
                    pool.sem_inc(y_free, 1)

            turns(turn)(pool)
            after(pool, scattered, E - 1, 16)

        @block.scalar
        def _(act):
            def turn(e, b, h):
                if has(e - 2):
                    after(act, down_done, e - 2)
                    act.wait_ge(y_free, e - 1)
                    act.copy(s.y_sb[b][:, 0:512], ps[:, 2, :]).then_inc(y_ready[0], 1)
                split_hi(act, e, b, h, -1, 4)
                split_hi(act, e, b, h, 1, 0)
                split_hi(act, e, b, h, -1, 5)
                if has(e - 1):
                    after(act, hid_turned, e - 1)
                    after(act, down_done, e - 2)
                    act.copy(s.hidT_hi[:], ps[:, 6, :].rearrange("p (c q) -> p c q", q=P)).then_inc(hT_hi_ready, 1)
                split_hi(act, e, b, h, 1, 1)
                split_hi(act, e, b, h, 1, 2)
                if has(e + 1):
                    after(act, rows_turned, e + 1)
                    after(act, gated, e - 1)
                    act.copy(as_banks(s.rT_hi[1 - b][:]), banks45).then_inc(rT_hi_ready, 1)
                split_hi(act, e, b, h, 1, 3)
                if has(e):
                    after(act, gated, e)
                    after(act, hid_ready, e - 1)
                    act.activation(s.silu[:], ps[:, 0, :], ACT.Silu).then_inc(silu_ready, 1)

            turns(turn)(act)

        @block.vector
        def _(dve):
            def turn(e, b, h):
                if has(e - 2):
                    after(dve, down_done, e - 2)
                    dve.wait_ge(y_free, e - 1)
                    dve.tensor_copy(s.idx_s[b][:], s.table[:, bass.ds(e - 2, 1), 0]).then_inc(scatter_idx, 1)
                    dve.tensor_copy(s.y_sb[b][:, 512:1024], ps[:, 3, :]).then_inc(y_ready[1], 1)
                if has(e + 2):
                    rows_loaded(dve, e, b, h, 0)
                    dve.tensor_copy(s.idx_g[b][:], s.table[:, bass.ds(e + 2, 1), 0]).then_inc(gather_idx, 1)
                split_lo(dve, e, b, -1, 4)
                split_lo(dve, e, b, 1, 0)
                if has(e - 1):
                    after(dve, hT_hi_ready, e - 1)
                    dve.tensor_tensor(s.hidT_lo[:], ps[:, 6, :].rearrange("p (c q) -> p c q", q=P),
                                      s.hidT_hi[:].bitcast(F32), ALU.subtract).then_inc(hT_lo_ready, 1)
                split_lo(dve, e, b, 1, 1)
                split_lo(dve, e, b, 1, 2)
                if has(e + 1):
                    after(dve, rT_hi_ready, e + 1)
                    dve.tensor_tensor(as_banks(s.rT_lo[1 - b][:]), banks45, as_banks(s.rT_hi[1 - b][:]).bitcast(F32),
                                      ALU.subtract).then_inc(rT_lo_ready, 1)
                split_lo(dve, e, b, 1, 3)
                if has(e):
                    after(dve, hid_ready, e - 2)
                    dve.tensor_copy(s.w_slot[b][:], s.table[:, bass.ds(e, 1), 1].bitcast(F32)).then_inc(weight_ready, 1)
                    after(dve, silu_ready, e)
                    after(dve, weight_ready, e)
                    after(dve, hid_turned, e - 2)
                    dve.scalar_tensor_tensor(s.hid[b][:].rearrange("s c p -> s p c"),
                                             s.silu[:].rearrange("s (p c) -> s p c", c=FC), s.w_slot[b][:],
                                             ps[:, 1, :].rearrange("s (p c) -> s p c", c=FC),
                                             ALU.mult, ALU.mult).then_inc(hid_ready, 1)

            turns(turn)(dve)

        @block.tensor
        def _(pe):
            def gate_up(e, b, q):
                if not has(e):
                    return
                if q == 0:
                    after(pe, rT_lo_ready, e)
                    after(pe, hid_ready, e - 1)
                after(pe, lo_ready[q], e)
                hi = s.w_hi[q][:].rearrange("p (g c n) -> p g c n", g=2, c=2)
                lo = s.w_lo[b][q][:].rearrange("p (g c n) -> p g c n", g=2, c=2)
                for c2 in range(2):
                    c = 2 * q + c2
                    for g in range(2):
                        pe.matmul(ps[:, g, :], s.rT_hi[b][:, c, :], hi[:, g, c2, :], start=(c == 0), stop=False)
                    for g in range(2):
                        pe.matmul(ps[:, g, :], s.rT_hi[b][:, c, :], lo[:, g, c2, :], start=False, stop=False)
                    for g in range(2):
                        ins = pe.matmul(ps[:, g, :], s.rT_lo[b][:, c, :], hi[:, g, c2, :], start=False, stop=(c == KC - 1))
                ins.then_inc(used[q], 1)
                if q == 3:
                    pe.wait_ge(used[q], (e + 1))
                    pe.sem_inc(gated, 1)

            def down(e, b, q):
                if not has(e):
                    return
                if q == 0:
                    after(pe, hT_lo_ready, e)
                    for n in range(2):
                        after(pe, y_ready[n], e - 1)
                after(pe, lo_ready[4 + q], e)
                hi = s.w_hi[4 + q][:].rearrange("p (c n) -> p c n", c=2)
                lo = s.w_lo[b][4 + q][:].rearrange("p (c n) -> p c n", c=2)
                for c2 in range(2):
                    c = 2 * q + c2
                    for n in range(2):
                        pe.matmul(ps[:, 2 + n, :], s.hidT_hi[:, c, :], hi[:, c2, n * 512:(n + 1) * 512], start=(c == 0), stop=False)
                    for n in range(2):
                        pe.matmul(ps[:, 2 + n, :], s.hidT_hi[:, c, :], lo[:, c2, n * 512:(n + 1) * 512], start=False, stop=False)
                    for n in range(2):
                        ins = pe.matmul(ps[:, 2 + n, :], s.hidT_lo[:, c, :], hi[:, c2, n * 512:(n + 1) * 512], start=False, stop=(c == FC - 1))
                ins.then_inc(used[4 + q], 1)
                if q == 1:
                    pe.wait_ge(used[4 + q], (e + 1))
                    pe.sem_inc(down_done, 1)

            def turn(e, b, h):
                gate_up(e, b, 0)
                gate_up(e, b, 1)
                if has(e - 1):
                    after(pe, hid_ready, e - 1)
                    after(pe, hT_lo_ready, e - 2)
                    for c in range(FC):
                        ins = pe.transpose(ps[:, 6, c * P:(c + 1) * P], s.hid[1 - b][:, c, :], s.ident[:])
                    ins.then_inc(hid_turned, 1)
                gate_up(e, b, 2)
                if has(e + 1):
                    rows_loaded(pe, e, b, h, 1)
                    after(pe, rT_lo_ready, e)
                    for c in range(KC):
                        ins = pe.transpose(ps[:, 4 + c // 4, (c % 4) * P:(c % 4 + 1) * P], s.rows[1 - b][:, c, :], s.ident[:])
                    ins.then_inc(rows_turned, 1)
                gate_up(e, b, 3)
                down(e - 1, 1 - b, 0)
                down(e - 1, 1 - b, 1)

            turns(turn)(pe)

    x = Shared()
    x.scattered, x.gather_idx, x.waited, x.rows_in, x.y_ready = scattered, gather_idx, waited, rows_in, y_ready
    x.gated, x.silu_ready, x.weight_ready, x.rows_turned, x.rT_hi_ready = gated, silu_ready, weight_ready, rows_turned, rT_hi_ready
    x.hid_ready, x.hid_turned, x.hT_hi_ready, x.down_done = hid_ready, hid_turned, hT_hi_ready, down_done
    spare_blocks(nc, s, x)


def spare_blocks(nc, s, x):
    ps = s.ps

    def each(eng, body):
        n = eng.value_load(s.spare_n[0:1, 0:1], min_val=0, max_val=SPARE)
        with eng.Fori(0, SPARE) as i:
            with eng.If(n > i):
                body(i)
        eng.nop()

    def before_done(eng, i):
        eng.wait_ge(x.scattered, i * 16 + E * 16)

    with nc.Block() as block:
        @block.sync
        def _(sp):
            def body(i):
                before_done(sp, i)
                e = sp.value_load(s.spare_e[0:1, bass.ds(i, 1)], min_val=0, max_val=E - 1)
                for q in range(4):
                    s.load_gate_up(sp, e, 0, q)
                for q in range(2):
                    s.load_down(sp, e, 0, q)

            each(sp, body)

        @block.gpsimd
        def _(pool):
            last_row = pool.to_reg(T - 1)

            def body(i):
                pool.wait_ge(x.gather_idx, i + (E + 1))
                pool.sem_inc(x.waited, 1)
                pool.indirect_dma_start(
                    out=s.rows[0][:].rearrange("p c q -> p (c q)"), out_offset=None, in_=s.xn2_rows,
                    in_offset=bass.IndirectOffsetOnAxis(ap=s.idx_g[0][:, 0:1], axis=0),
                    bounds_check=last_row, oob_is_err=False).then_inc(x.rows_in[0], 16)
                pool.wait_ge(x.y_ready[0], i + (E + 1))
                pool.sem_inc(x.waited, 1)
                pool.indirect_dma_start(
                    out=s.out_rows, out_offset=bass.IndirectOffsetOnAxis(ap=s.idx_g[0][:, 0:1], axis=0),
                    in_=s.y_sb[0][:], in_offset=None, bounds_check=last_row, oob_is_err=False,
                    compute_op=ALU.add).then_inc(x.scattered, 16)
                before_done(pool, i + 1)

            each(pool, body)

        @block.scalar
        def _(act):
            def body(i):
                act.wait_ge(x.gated, i + (E + 1))
                act.activation(s.silu[:], ps[:, 0, :], ACT.Silu).then_inc(x.silu_ready, 1)

            each(act, body)

        @block.vector
        def _(dve):
            def body(i):
                before_done(dve, i)
                dve.tensor_copy(s.idx_g[0][:], s.table[:, bass.ds(i + E, 1), 0]).then_inc(x.gather_idx, 1)
                dve.tensor_copy(s.w_slot[0][:], s.table[:, bass.ds(i + E, 1), 1].bitcast(F32)).then_inc(x.weight_ready, 1)
                dve.wait_ge(x.rows_turned, i + (E + 1))
                dve.tensor_copy(s.spare_xT[:].rearrange("p (a c) q -> p a (c q)", a=2), ps[:, 4:6, :]).then_inc(x.rT_hi_ready, 1)
                dve.wait_ge(x.silu_ready, i + (E + 1))
                dve.wait_ge(x.weight_ready, i + (E + 1))
                dve.scalar_tensor_tensor(s.hid[0][:].rearrange("s c p -> s p c"),
                                         s.silu[:].rearrange("s (p c) -> s p c", c=FC), s.w_slot[0][:],
                                         ps[:, 1, :].rearrange("s (p c) -> s p c", c=FC),
                                         ALU.mult, ALU.mult).then_inc(x.hid_ready, 1)
                dve.wait_ge(x.hid_turned, i + (E + 1))
                dve.tensor_copy(s.spare_hT[:], ps[:, 6, :].rearrange("p (c q) -> p c q", q=P)).then_inc(x.hT_hi_ready, 1)
                dve.wait_ge(x.down_done, i + (E + 1))
                dve.tensor_copy(s.y_sb[0][:].rearrange("p (a n) -> p a n", a=2), ps[:, 2:4, :]).then_inc(x.y_ready[0], 1)

            each(dve, body)

        @block.tensor
        def _(pe):
            def body(i):
                pe.wait_ge(x.rows_in[0], i * 16 + 16 * (E // 2 + 1))
                for c in range(KC):
                    ins = pe.transpose(ps[:, 4 + c // 4, (c % 4) * P:(c % 4 + 1) * P], s.rows[0][:, c, :], s.ident[:])
                ins.then_inc(x.rows_turned, 1)
                pe.wait_ge(x.rT_hi_ready, i + (E + 1))
                for c in range(KC):
                    pe.wait_ge(s.loaded[0][c // 2], i * 32 + 32 * (E // 2 + 1))
                    w = s.raw[0][c // 2][:].rearrange("p (g c n) -> p g c n", g=2, c=2)
                    for g in range(2):
                        ins = pe.matmul(ps[:, g, :], s.spare_xT[:, c, :], w[:, g, c % 2, :], start=(c == 0), stop=(c == KC - 1))
                ins.then_inc(x.gated, 1)
                pe.wait_ge(x.hid_ready, i + (E + 1))
                for c in range(FC):
                    ins = pe.transpose(ps[:, 6, c * P:(c + 1) * P], s.hid[0][:, c, :], s.ident[:])
                ins.then_inc(x.hid_turned, 1)
                pe.wait_ge(x.hT_hi_ready, i + (E + 1))
                for c in range(FC):
                    pe.wait_ge(s.loaded[0][4 + c // 2], i * 16 + 16 * (E // 2 + 1))
                    w = s.raw[0][4 + c // 2][:].rearrange("p (c n) -> p c n", c=2)
                    for n in range(2):
                        ins = pe.matmul(ps[:, 2 + n, :], s.spare_hT[:, c, :], w[:, c % 2, n * 512:(n + 1) * 512],
                                        start=(c == 0), stop=(c == FC - 1))
                ins.then_inc(x.down_done, 1)

            each(pe, body)


_INS = ["x", "positions", "attn_norm_gain", "w_in", "q_norm_gain", "k_norm_gain", "lambda_q1",
        "lambda_k1", "lambda_q2", "lambda_k2", "subln_gain", "conv_w", "conv_out_gain", "w_out",
        "ffn_norm_gain", "w_group_router", "w_expert_router", "w_gate", "w_up", "w_down"]


def kernel(**inputs):
    import numpy as _np
    import concourse.bacc as _bacc
    from concourse import mybir as _mybir
    from concourse.bass_utils import run_bass_kernel_spmd as _run

    nc = _bacc.Bacc("TRN2", target_bir_lowering=False, num_devices=1)
    arrays, args = {}, []
    for name in _INS:
        a = _np.ascontiguousarray(inputs[name])
        arrays[f"in_{name}"] = a
        args.append(nc.dram_tensor(f"in_{name}", a.shape, _mybir.dt.from_np(a.dtype), kind="ExternalInput").ap())
    args.append(nc.dram_tensor("out_0", (1, T, D), _mybir.dt.float32, kind="ExternalOutput").ap())
    layer_kernel(nc, *args)
    r = _run(nc, [arrays], core_ids=[0])
    return r.results[0]["out_0"]
```

```python
from contextlib import ExitStack

import concourse.bass as bass
from concourse import mybir

F32 = mybir.dt.float32
F32R = mybir.dt.float32r
BF16 = mybir.dt.bfloat16
U32 = mybir.dt.uint32
I32 = mybir.dt.int32
ALU = mybir.AluOpType
ACT = mybir.ActivationFunctionType
AX = mybir.AxisListType

P = 128
T = 1024
D = 1024
NT = T // P
KC = D // P
HEADS = 4
DV = 128
DK = 64
PIECES = 4
CONV = 512
CT = CONV // P
ROT = 16
THETA = 500000.0
EPS = 1e-6
GROUPS = 4
PER_GROUP = 8
E = GROUPS * PER_GROUP
FF = 512
FC = FF // P
TOP_K = 2
COL_Q, COL_K, COL_V, COL_B, COL_C, COL_U = 0, 512, 1024, 1536, 2048, 2560
LAMBDA_INIT = 0.2
MASKED = -1e30
SLOTS = 96
MORE = (T - 1) // SLOTS
SPARE = (T * TOP_K - E) // SLOTS
BLOCKS = E + SPARE
NO_TOKEN = T

KB = 1024


class Shared:
    pass


class Order:

    def __init__(self, eng, sem):
        self.eng, self.sem, self.n, self.start, self.i, self.steps = eng, sem, 0, 0, None, 0

    def value(self, n):
        return self.start + n if self.i is None else self.i * self.steps + (self.start + n)

    def mark(self, ins):
        ins.then_inc(self.sem, 1)
        self.n += 1
        return self.n

    def wait(self, n):
        self.eng.wait_ge(self.sem, self.value(n))

    def then(self, ins):
        self.wait(self.mark(ins))

    def enter(self, i, steps):
        self.start, self.n, self.i, self.steps = self.start + self.n, 0, i, steps

    def leave(self, times):
        assert self.n == self.steps, (self.n, self.steps)
        self.start, self.n, self.i = self.start + times * self.steps, 0, None


def layer_kernel(nc, x, positions, attn_norm_gain, w_in, q_norm_gain, k_norm_gain, lambda_q1,
                 lambda_k1, lambda_q2, lambda_k2, subln_gain, conv_w, conv_out_gain, w_out,
                 ffn_norm_gain, w_group_router, w_expert_router, w_gate, w_up, w_down, out):
    ctx = ExitStack()
    with ctx:
        base = nc.sbuf_base
        slab = 207 * KB
        ctx.enter_context(nc.sbuf_tensor("slab", [P, slab], mybir.dt.uint8))
        base = -(-base // 32) * 32

        def at(name, kb, shape, dtype=F32):
            return nc.alloc_sbuf_tensor_at(name, shape, dtype, offset=base + int(kb * KB))

        ps = ctx.enter_context(nc.psum_tensor("banks", [P, 8, 512], F32))

        def sem(name):
            return ctx.enter_context(nc.semaphore(name))

        xn2_rows = nc.dram_tensor("xn2_rows", [T, D], F32, kind="Internal").ap()

        out_rows = out.rearrange("b t d -> (b t) d")
        x_rows = x.rearrange("b t d -> (b t) d")

        ident = at("ident", 0, [P, P])
        ident_b = at("ident_b", 0.5, [P, P], BF16)
        causal_b = at("causal_b", 0.75, [P, P], BF16)
        before_b = at("before_b", 1, [P, P], BF16)
        ones_b = at("ones_b", 1.25, [P, P], BF16)
        cos2 = at("cos2", 1.5, [P, NT, ROT])
        sin2 = at("sin2", 2, [P, NT, ROT])
        qk_gain = at("qk_gain", 2.5, [P, 2, 2, DK])
        conv_taps = at("conv_taps", 3.5, [P, CT, 4])
        sub_gain = at("sub_gain", 3.625, [P, 1])
        neg_lam = at("neg_lam", 3.65625, [P, 1])
        neg_half = at("neg_half", 3.6875, [P, NT])
        ones_col = at("ones_col", 3.71875, [P, 1])
        eps_qk = at("eps_qk", 3.75, [P, NT])
        eps_o = at("eps_o", 3.78125, [P, 1])
        rstd_c = at("rstd_c", 4, [P, NT])
        pos_i = at("pos_i", 4.03125, [P, NT], I32)
        rstd_x = at("rstd_x", 4.0625, [P, NT])
        ss_x = at("ss_x", 4.09375, [P, NT])
        ang = at("ang", 4.125, [P, NT, 8])
        angc = at("angc", 4.375, [P, NT, 8])
        turns = at("turns", 4.625, [P, NT, 8])
        lam4 = at("lam4", 5, [P, 4, DK])
        lamt = at("lamt", 6, [P, DK])
        posf = at("posf", 6.25, [P, NT])
        freqs = at("freqs", 6.3125, [P, 8])
        lamd = at("lamd", 6.375, [P, 4])

        xT_hi = at("xT_hi", 8, [P, KC, T], F32R)
        xT_lo = at("xT_lo", 40, [P, KC, T], F32R)
        mixT = at("mixT", 72, [P, KC, T])

        x_all = at("x_all", 104, [P, NT, D])
        xn = [at(f"xn{b}", 136 + 4 * b, [P, D]) for b in range(2)]
        gain1 = at("gain1", 144, [P, D])
        squares = at("squares", 148, [P, D])

        z_raw = [at(f"z_raw{s}", 160 + 4 * s, [P, KC, P]) for s in range(2)]
        z_hi = [at(f"z_hi{s}", 168 + 4 * s, [P, KC, P], F32R) for s in range(2)]
        z_lo = [at(f"z_lo{s}", 176 + 4 * s, [P, KC, P], F32R) for s in range(2)]
        c_sb = at("c_sb", 184, [P, T])
        cu = at("cu", 188, [P, T + 2])
        z_taps = at("z_taps", 193, [P, 4])

        q_raw = at("q_raw", 104, [P, KC, 3, P])
        b_raw = at("b_raw", 116, [P, KC, P])
        q_hi = at("q_hi", 120, [P, KC, 3 * P], F32R)
        q_lo = at("q_lo", 132, [P, KC, 3 * P], F32R)
        b_hi = at("b_hi", 144, [P, KC, P], F32R)
        b_lo = at("b_lo", 148, [P, KC, P], F32R)
        q_stack = at("q_stack", 152, [P, 2, T], F32R)
        k_hi = at("k_hi", 160, [P, 2, T], F32R)
        k_lo = at("k_lo", 168, [P, 2, T], F32R)
        v_sb = at("v_sb", 176, [P, NT, DV])
        probs = [at("probs0", 180, [P, 2, T - P]), at("probs1", 187, [P, 2, T])]
        mapsT = [at("mapsT0", 195, [P, NT - 1, P]), at("mapsT1", 198.5, [P, NT, P])]
        conv_sq = at("conv_sq", 202.5, [P, T])
        qk_scaled = [at(f"qk_scaled{b}", 180 + b, [P, 4, DK]) for b in range(2)]
        qk_twice = [at(f"qk_twice{b}", 182 + 2 * b, [P, 4, 2, DK]) for b in range(2)]
        rot_a = at("rot_a", 186, [P, 4, ROT])
        rot_b = at("rot_b", 186.25, [P, 4, ROT])
        qk_sq = at("qk_sq", 186.5, [P, 4, DK])
        bz = at("bz", 144, [P, T])
        bz_sq = at("bz_sq", 148, [P, T])
        g_taps = at("g_taps", 206.5, [P, 4])
        qk_ss = at("qk_ss", 206.53125, [P, 2, 4])
        qk_rstd = at("qk_rstd", 206.5625, [P, 2, 4])
        neg_max = at("neg_max", 206.59375, [P, 2, 2])
        sums = at("sums", 206.625, [P, 8, 2])
        inv_sums = at("inv_sums", 206.6875, [P, 8, 2])
        ratio = at("ratio", 206.75, [P, 2])
        o_ss = at("o_ss", 206.78125, [P, 2])
        o_rstd = at("o_rstd", 206.8125, [P, 2])
        neg_one = at("neg_one", 6.4375, [P, 2])
        o_sb = [at(f"o_sb{b}", 6.5 + 0.5 * b, [P, DV]) for b in range(2)]
        o_sq = at("o_sq", 5, [P, DV])

        wo_hi = at("wo_hi", 8, [P, KC, D], F32R)
        wo_lo = at("wo_lo", 40, [P, KC, D], F32R)
        wo_raw = at("wo_raw", 40, [P, KC, D])
        m_hi = [at(f"m_hi{b}", 112 + 4 * b, [P, KC, P], F32R) for b in range(2)]
        m_lo = [at(f"m_lo{b}", 120 + 4 * b, [P, KC, P], F32R) for b in range(2)]
        x_again = [at(f"x_again{b}", 128 + 4 * b, [P, D]) for b in range(2)]
        h_sb = [at(f"h_sb{b}", 136 + 4 * b, [P, D]) for b in range(2)]
        hn = [at(f"hn{b}", 144 + 4 * b, [P, KC, P]) for b in range(2)]
        hnT = at("hnT", 152, [P, KC, P])
        h_sq = at("h_sq", 156, [P, D])
        gain2 = at("gain2", 160, [P, D])
        w_route = at("w_route", 164, [P, KC, GROUPS + E])
        logits = at("logits", 166, [P, NT, GROUPS + E])
        logitsT = at("logitsT", 172, [GROUPS + E, T])
        h_ss = at("h_ss", 168, [P, 2])
        h_rstd = at("h_rstd", 168.0625, [P, 2])

        raw = [[at(f"raw{b}_{k}", 56 - 48 * b + 8 * k, [P, 2048]) for k in range(6)] for b in range(2)]
        w_lo = [[at(f"wlo{b}_{k}", 56 - 48 * b + 8 * k, [P, 2048], F32R) for k in range(6)]
                for b in range(2)]
        w_hi = [at(f"whi{k}", 104 + 8 * k, [P, 2048], F32R) for k in range(6)]
        rows = [at(f"rows{b}", 152 + 4 * b, [SLOTS, KC, P]) for b in range(2)]
        rT_hi = [at(f"rT_hi{b}", 160 + 4 * b, [P, KC, SLOTS], F32R) for b in range(2)]
        rT_lo = [at(f"rT_lo{b}", 168 + 4 * b, [P, KC, SLOTS], F32R) for b in range(2)]
        hid = [at(f"hid{b}", 176 + 2 * b, [SLOTS, FC, P]) for b in range(2)]
        hidT_hi = at("hidT_hi", 180, [P, FC, SLOTS], F32R)
        hidT_lo = at("hidT_lo", 182, [P, FC, SLOTS], F32R)
        silu = at("silu", 184, [SLOTS, FF])
        y_sb = [at(f"y_sb{b}", 186 + 4 * b, [SLOTS, D]) for b in range(2)]
        table = at("table", 194, [SLOTS, BLOCKS, 2], U32)
        spare_xT = at("spare_xT", 195, [P, KC, SLOTS])
        spare_hT = at("spare_hT", 199, [P, FC, SLOTS])
        idx_g = [at(f"idx_g{b}", 201 + 0.0625 * b, [SLOTS, 1], U32) for b in range(2)]
        idx_s = [at(f"idx_s{b}", 201.125 + 0.0625 * b, [SLOTS, 1], U32) for b in range(2)]
        w_slot = [at(f"w_slot{b}", 201.25 + 0.0625 * b, [SLOTS, 1]) for b in range(2)]
        spare_n = at("spare_n", 201.5, [P, 1], I32)
        spare_e = at("spare_e", 201.5625, [P, SPARE], I32)

        kept = [[1.5, 8.0]]
        iota_e = place(at, kept, "iota_e", [P, E])
        iota_r = place(at, kept, "iota_r", [P, SLOTS])
        iota_b = place(at, kept, "iota_b", [P, SPARE])
        full = place(at, kept, "full", [P, MORE])
        tok = place(at, kept, "tok", [P, NT])
        ones_e = place(at, kept, "ones_e", [P, E])
        weight = place(at, kept, "weight", [P, TOP_K, NT])
        slot = place(at, kept, "slot", [P, TOP_K, NT])
        own_e = place(at, kept, "own_e", [P, TOP_K, NT])
        cnt = place(at, kept, "cnt", [P, E])

        small_in = sem("small_in")
        gain1_in = sem("gain1_in")
        x_in = [sem(f"x_in{t}") for t in range(NT // 2)]
        z_raw_in = [sem(f"z_raw_in{s}") for s in range(2)]
        consts = sem("consts")
        squared = sem("squared")
        z_lo_ready = [sem(f"z_lo_ready{s}") for s in range(2)]
        z_hi_ready = [sem(f"z_hi_ready{s}") for s in range(2)]
        pool_own = sem("pool_own")
        dve_own = sem("dve_own")
        rstd_ready = sem("rstd_ready")
        xn_ready = sem("xn_ready")
        xn_turned = sem("xn_turned")
        xhi_ready = sem("xhi_ready")
        xlo_ready = sem("xlo_ready")
        angles_ready = sem("angles_ready")
        tables_ready = sem("tables_ready")
        lam_dots = sem("lam_dots")
        lam_exp = sem("lam_exp")
        w_in_pc = w_in[0].rearrange("(c p) n -> p c n", p=P)

        with nc.Block() as block:
            @block.sync
            def _(sp):
                for t in range(0, NT, 2):
                    sp.dma_start(x_all[:, t:t + 2, :], x_rows[t * P:(t + 2) * P, :].rearrange("(a p) d -> p a d", p=P)).then_inc(x_in[t // 2], 16)
                    if t == 0:
                        sp.dma_start(gain1[:], attn_norm_gain[0:1, :].to_broadcast([P, D])).then_inc(gain1_in, 16)
                for s, col in ((0, COL_C), (1, COL_U)):
                    sp.dma_start(z_raw[s][:], w_in_pc[:, :, col:col + P]).then_inc(z_raw_in[s], 16)
                with nc.allow_non_contiguous_dma(reason="positions and gains, a few hundred words"):
                    sp.dma_start(pos_i[:], positions[0].rearrange("(t p) -> p t", p=P)).then_inc(small_in, 16)
                    for m, g in enumerate((q_norm_gain, k_norm_gain)):
                        for n in range(2):
                            sp.dma_start(qk_gain[:, m, n, :], g[0:1, :].to_broadcast([P, DK])).then_inc(small_in, 16)
                    for j, g in enumerate((lambda_q1, lambda_k1, lambda_q2, lambda_k2)):
                        sp.dma_start(lam4[:, j, :], g[0:1, :].to_broadcast([P, DK])).then_inc(small_in, 16)
                    for m in range(CT):
                        sp.dma_start(conv_taps[:, m, 0:3], conv_w[0][:, m * P:(m + 1) * P].rearrange("j p -> p j")).then_inc(small_in, 16)
                    sp.dma_start(conv_taps[:, :, 3], conv_out_gain[0].rearrange("(m p) -> p m", p=P)).then_inc(small_in, 16)
                    sp.dma_start(sub_gain[:], subln_gain.rearrange("a p -> p a")).then_inc(small_in, 16)

            @block.gpsimd
            def _(pool):
                own = Order(pool, pool_own)
                pool.memset(neg_half[:], -0.5).then_inc(consts, 1)
                pool.memset(ones_col[:], 1.0).then_inc(consts, 1)
                pool.memset(neg_one[:], -1.0).then_inc(consts, 1)
                pool.memset(eps_qk[:], EPS).then_inc(consts, 1)
                pool.memset(eps_o[:], EPS * DV).then_inc(consts, 1)
                pool.memset(conv_sq[:], 0.0).then_inc(consts, 1)
                pool.memset(ones_b[:], 1.0).then_inc(consts, 1)
                own.mark(pool.memset(ident[:], 0.0))
                own.mark(pool.memset(ident_b[:], 0.0))
                own.mark(pool.memset(causal_b[:], 0.0))
                own.then(pool.memset(before_b[:], 1.0))
                pool.affine_select(out=ident[:], in_=ident[:], compare_op=ALU.not_equal, fill=1.0, base=0,
                                   pattern=[[-1, P]], channel_multiplier=1).then_inc(consts, 1)
                pool.affine_select(out=ident_b[:], in_=ident_b[:], compare_op=ALU.not_equal, fill=1.0, base=0,
                                   pattern=[[-1, P]], channel_multiplier=1).then_inc(consts, 1)
                pool.affine_select(out=causal_b[:], in_=causal_b[:], compare_op=ALU.is_ge, fill=MASKED, base=0,
                                   pattern=[[-1, P]], channel_multiplier=1).then_inc(consts, 1)
                pool.affine_select(out=before_b[:], in_=before_b[:], compare_op=ALU.is_gt, fill=0.0, base=0,
                                   pattern=[[1, P]], channel_multiplier=-1).then_inc(consts, 1)
                for j in range(NT // 2):
                    two = slice(2 * j, 2 * j + 2)
                    pool.wait_ge(squared, 2 * j + 2)
                    own.then(pool.tensor_scalar(ss_x[:, two], ss_x[:, two], 1.0 / D, EPS, ALU.mult, ALU.add))
                    pool.tensor_tensor(rstd_x[:, two], ss_x[:, two], neg_half[:, two], ALU.pow).then_inc(rstd_ready, 1)
                for s in range(2):
                    pool.wait_ge(z_hi_ready[s], 1)
                    pool.tensor_tensor(z_lo[s][:], z_raw[s][:], z_hi[s][:].bitcast(F32), ALU.subtract).then_inc(z_lo_ready[s], 1)

            @block.scalar
            def _(act):
                def square(t):
                    act.wait_ge(x_in[t // 2], 16)
                    if t >= 1:
                        act.wait_ge(squared, t)
                    act.activation(squares[:], x_all[:, t, :], ACT.Square,
                                   accum_out=ss_x[:, t:t + 1]).then_inc(squared, 1)

                for t in range(4):
                    square(t)
                for t in range(NT):
                    b = t % 2
                    act.wait_ge(xn_turned, t + 1)
                    act.copy(xT_hi[:, :, t * P:(t + 1) * P].rearrange("p (a c) q -> p a c q", a=2),
                             ps[:, 2 * b:2 * b + 2, :].rearrange("p a (c q) -> p a c q", q=P)).then_inc(xhi_ready, 1)
                    if t + 4 < NT:
                        square(t + 4)
                    if t in (4, 5):
                        act.wait_ge(z_raw_in[t - 4], 16)
                        act.copy(z_hi[t - 4][:], z_raw[t - 4][:]).then_inc(z_hi_ready[t - 4], 1)

            @block.vector
            def _(dve):
                own = Order(dve, dve_own)
                own.mark(dve.memset(cu[:, 0:2], 0.0))
                for j in range(8):
                    own.mark(dve.memset(freqs[:, j:j + 1], float(THETA) ** (-(2 * j) / ROT)))
                dve.wait_ge(gain1_in, 16)

                def scale(t, b):
                    dve.wait_ge(rstd_ready, t // 2 + 1)
                    dve.scalar_tensor_tensor(xn[b][:], x_all[:, t, :], rstd_x[:, t:t + 1], gain1[:],
                                             ALU.mult, ALU.mult).then_inc(xn_ready, 1)

                for t in range(NT):
                    if t >= 2:
                        dve.wait_ge(xn_turned, t - 1)
                    scale(t, t % 2)
                    if t >= 1:
                        low_half(nc, dve, t - 1, xhi_ready, xT_hi, xT_lo, ps, xlo_ready)
                low_half(nc, dve, NT - 1, xhi_ready, xT_hi, xT_lo, ps, xlo_ready)

            @block.tensor
            def _(pe):
                pe.wait_ge(consts, 11)
                for t in range(NT):
                    b = t % 2
                    pe.wait_ge(xn_ready, t + 1)
                    if t >= 2:
                        pe.wait_ge(xlo_ready, t - 1)
                    for c in range(KC):
                        ins = pe.transpose(ps[:, 2 * b + c // 4, (c % 4) * P:(c % 4 + 1) * P],
                                           xn[b][:, c * P:(c + 1) * P], ident[:])
                    ins.then_inc(xn_turned, 1)

        z_multiplied = [sem(f"z_multiplied{s}") for s in range(2)]
        c_copied = sem("c_copied")
        cu_ready = sem("cu_ready")
        q_in = sem("q_in")
        wo_in = sem("wo_in")
        projected = sem("projected")
        b_in = sem("b_in")
        dve_own2 = sem("dve_own2")

        b_hi_ready = sem("b_hi_ready")
        b_lo_ready = sem("b_lo_ready")
        q_hi_ready = sem("q_hi_ready")
        q_lo_ready = sem("q_lo_ready")

        def load_q(sp, h):
            for j, col in enumerate((COL_Q, COL_K, COL_V)):
                sp.dma_start(q_raw[:, :, j, :], w_in_pc[:, :, bass.ds(h * P + col, P)]).then_inc(q_in, 16)

        def load_b(sp, h):
            sp.dma_start(b_raw[:], w_in_pc[:, :, bass.ds(h * P + COL_B, P)]).then_inc(b_in, 16)

        def project(pe, h, i):
            cols = slice(i * P, (i + 1) * P)
            o = ps[:, 2 + i % 4, 0:3 * P]
            for c in range(KC):
                pe.matmul(o, xT_hi[:, c, cols], q_hi[:, c, :], start=(c == 0), stop=False)
                pe.matmul(o, xT_hi[:, c, cols], q_lo[:, c, :], start=False, stop=False)
                ins = pe.matmul(o, xT_lo[:, c, cols], q_hi[:, c, :], start=False, stop=(c == KC - 1))
            ins.then_inc(projected, 1)

        def piece(a, n):
            return a[:, n * (KC // PIECES):(n + 1) * (KC // PIECES)]

        def round_q(act, n):
            act.copy(piece(q_hi, n), piece(q_raw, n).rearrange("p c j n -> p c (j n)")).then_inc(q_hi_ready, 1)

        def low_q(pool, n, count):
            pool.wait_ge(q_hi_ready, count)
            pool.tensor_tensor(piece(q_lo, n), piece(q_raw, n).rearrange("p c j n -> p c (j n)"),
                               piece(q_hi, n).bitcast(F32), ALU.subtract).then_inc(q_lo_ready, 1)

        with nc.Block() as block:
            @block.sync
            def _(sp):
                load_q(sp, 0)
                load_b(sp, 0)
                with sp.Fori(0, CT - 1) as m:
                    for s, col in ((0, COL_C), (1, COL_U)):
                        sp.wait_ge(z_lo_ready[s], m + 1)
                        sp.dma_start(z_raw[s][:], w_in_pc[:, :, bass.ds(m * P + (col + P), P)]).then_inc(z_raw_in[s], 16)

            @block.scalar
            def _(act):
                def copy_c(m):
                    act.wait_ge(z_multiplied[0], m + 2)
                    act.wait_ge(cu_ready, m + 1)
                    act.copy(c_sb[:], ps[:, 0:2, :]).then_inc(c_copied, 1)

                with act.Fori(0, CT - 1) as m:
                    copy_c(m)
                    for s in range(2):
                        act.wait_ge(z_raw_in[s], m * 16 + 32)
                        act.wait_ge(z_multiplied[s], m + 2)
                        act.copy(z_hi[s][:], z_raw[s][:]).then_inc(z_hi_ready[s], 1)
                copy_c(CT - 1)
                act.wait_ge(q_in, 48)
                for n in range(PIECES):
                    round_q(act, n)
                act.wait_ge(angles_ready, 1)
                act.activation(sin2[:, :, 8:16], ang[:], ACT.Sin).then_inc(tables_ready, 1)
                act.activation(cos2[:, :, 0:8], angc[:], ACT.Sin).then_inc(tables_ready, 1)
                act.wait_ge(lam_dots, 1)
                act.activation(lamd[:, 2:4], lamd[:, 0:2], ACT.Exp).then_inc(lam_exp, 1)

            @block.gpsimd
            def _(pool):
                with pool.Fori(0, CT - 1) as m:
                    for s in range(2):
                        pool.wait_ge(z_hi_ready[s], m + 2)
                        pool.tensor_tensor(z_lo[s][:], z_raw[s][:], z_hi[s][:].bitcast(F32),
                                           ALU.subtract).then_inc(z_lo_ready[s], 1)
                for n in range(PIECES):
                    low_q(pool, n, n + 1)

            @block.vector
            def _(dve):
                own = Order(dve, dve_own2)
                dve.sem_inc(cu_ready, 1)
                dve.wait_ge(small_in, 16 * 15)
                own.mark(dve.tensor_scalar(qk_gain[:, 0, :, :], qk_gain[:, 0, :, :], DK ** -0.5, None, ALU.mult))
                own.mark(dve.tensor_scalar(sub_gain[:], sub_gain[:], (1.0 - LAMBDA_INIT) * DV ** 0.5, None, ALU.mult))
                own.then(dve.tensor_copy(posf[:], pos_i[:]))
                own.then(dve.tensor_tensor(ang[:], posf[:].unsqueeze(2).to_broadcast([P, NT, 8]),
                                           freqs[:].unsqueeze(1).to_broadcast([P, NT, 8]), ALU.mult))
                ROUND = 12582912.0
                TWO_PI = (6.28125, 1.93500518798828125e-3, 3.0199159819567e-7)
                own.then(dve.tensor_scalar(turns[:], ang[:], 0.15915494309189535, 0.25, ALU.mult, ALU.add))
                own.then(dve.tensor_scalar(turns[:], turns[:], ROUND, None, ALU.add))
                own.then(dve.tensor_scalar(turns[:], turns[:], -ROUND, None, ALU.add))
                own.then(dve.scalar_tensor_tensor(angc[:], turns[:], -TWO_PI[0], ang[:], ALU.mult, ALU.add))
                for part in TWO_PI[1:]:
                    own.then(dve.scalar_tensor_tensor(angc[:], turns[:], -part, angc[:], ALU.mult, ALU.add))
                own.then(dve.tensor_scalar(angc[:], angc[:], 1.5707963267948966, 3.1415925, ALU.add, ALU.min))
                own.then(dve.tensor_scalar(angc[:], angc[:], -3.1415925, None, ALU.max))
                own.then(dve.tensor_scalar(turns[:], ang[:], 0.15915494309189535, None, ALU.mult))
                own.then(dve.tensor_scalar(turns[:], turns[:], ROUND, None, ALU.add))
                own.then(dve.tensor_scalar(turns[:], turns[:], -ROUND, None, ALU.add))
                for part in TWO_PI:
                    own.then(dve.scalar_tensor_tensor(ang[:], turns[:], -part, ang[:], ALU.mult, ALU.add))
                dve.tensor_scalar(ang[:], ang[:], 3.1415925, -3.1415925, ALU.min, ALU.max).then_inc(angles_ready, 1)
                own.then(dve.tensor_tensor_reduce(lamt[:], lam4[:, 0, :], lam4[:, 1, :], 1.0, 0.0, ALU.mult, ALU.add, lamd[:, 0:1]))
                dve.tensor_tensor_reduce(lamt[:], lam4[:, 2, :], lam4[:, 3, :], 1.0, 0.0, ALU.mult, ALU.add, lamd[:, 1:2]).then_inc(lam_dots, 1)
                with dve.Fori(0, CT) as m:
                    own.enter(m, 4)
                    own.mark(dve.tensor_copy(z_taps[:], conv_taps[:, bass.ds(m, 1), :]))
                    dve.wait_ge(c_copied, m + 2)
                    dve.wait_ge(z_multiplied[1], m + 2)
                    dve.tensor_tensor(cu[:, 2:T + 2].rearrange("p (a n) -> p a n", a=2), ps[:, 2:4, :],
                                      c_sb[:].rearrange("p (a n) -> p a n", a=2), ALU.mult).then_inc(cu_ready, 1)
                    dve.wait_ge(cu_ready, m + 2)
                    own.wait(1)
                    z = mixT[:, bass.ds(m + HEADS, 1), :].rearrange("p a t -> p (a t)")
                    own.then(dve.tensor_scalar(z, cu[:, 0:T], z_taps[:, 0:1], None, ALU.mult))
                    own.then(dve.scalar_tensor_tensor(z, cu[:, 1:T + 1], z_taps[:, 1:2], z, ALU.mult, ALU.add))
                    own.then(dve.scalar_tensor_tensor(z, cu[:, 2:T + 2], z_taps[:, 2:3], z, ALU.mult, ALU.add))
                    own.leave(CT)
                dve.wait_ge(lam_exp, 1)
                own.then(dve.tensor_tensor(neg_lam[:], lamd[:, 3:4], lamd[:, 2:3], ALU.subtract))
                own.mark(dve.tensor_scalar(neg_lam[:], neg_lam[:], -LAMBDA_INIT, None, ALU.add))
                dve.wait_ge(tables_ready, 2)
                own.mark(dve.tensor_copy(cos2[:, :, 8:16], cos2[:, :, 0:8]))
                own.then(dve.tensor_scalar(sin2[:, :, 0:8], sin2[:, :, 8:16], -1.0, None, ALU.mult))

            @block.tensor
            def _(pe):
                for s in range(2):
                    pe.sem_inc(z_multiplied[s], 1)
                pe.sem_inc(c_copied, 1)
                with pe.Fori(0, CT) as m:
                    for s in range(2):
                        pe.wait_ge(z_lo_ready[s], m + 1)
                        if s == 0:
                            pe.wait_ge(c_copied, m + 1)
                        else:
                            pe.wait_ge(cu_ready, m + 1)
                        ins = product_T(pe, ps, 2 * s, z_hi[s], z_lo[s], xT_hi, xT_lo)
                        ins.then_inc(z_multiplied[s], 1)
                pe.sem_inc(projected, 1)
                pe.wait_ge(q_lo_ready, PIECES)
                pe.wait_ge(cu_ready, CT + 1)
                for i in range(2):
                    project(pe, 0, i)

        table_parts = sem("table_parts")
        table_summed = sem("table_summed")
        loaded = [[sem(f"loaded{b}_{k}") for k in range(6)] for b in range(2)]

        hi_ready = [sem(f"hi_ready{k}") for k in range(6)]
        lo_ready = [sem(f"lo_ready{k}") for k in range(6)]

        def load_gate_up(eng, e, b, q, done=None):
            slot = raw[b][q][:].rearrange("p (g c n) -> p g c n", g=2, c=2)
            for g, w in enumerate((w_gate, w_up)):
                rows_of = w[0, bass.ds(e, 1)].rearrange("a (p c) n -> p (a c) n", c=KC)
                eng.dma_start(slot[:, g, :, :], rows_of[:, 2 * q:2 * q + 2, :]).then_inc(done or loaded[b][q], 16)

        def load_down(eng, e, b, q, done=None):
            rows_of = w_down[0, bass.ds(e, 1)].rearrange("a (p c) n -> p (a c) n", c=FC)
            eng.dma_start(raw[b][4 + q][:].rearrange("p (c n) -> p c n", c=2),
                          rows_of[:, 2 * q:2 * q + 2, :]).then_inc(done or loaded[b][4 + q], 16)

        s = Shared()
        s.ps, s.q_lo_ready, s.load_q, s.b_lo_ready, s.load_b = ps, q_lo_ready, load_q, b_lo_ready, load_b
        s.wo_raw, s.w_out, s.wo_in, s.projected, s.qk_sq = wo_raw, w_out, wo_in, projected, qk_sq
        s.v_sb, s.b_in, s.b_hi, s.b_raw, s.b_hi_ready = v_sb, b_in, b_hi, b_raw, b_hi_ready
        s.q_stack, s.k_hi, s.mapsT, s.probs, s.neg_max = q_stack, k_hi, mapsT, probs, neg_max
        s.sums, s.q_in, s.round_q, s.o_sq, s.inv_sums = sums, q_in, round_q, o_sq, inv_sums
        s.o_ss, s.mixT, s.sub_gain, s.qk_rstd, s.qk_ss = o_ss, mixT, sub_gain, qk_rstd, qk_ss
        s.eps_qk, s.neg_half, s.qk_twice, s.rot_a, s.cos2 = eps_qk, neg_half, qk_twice, rot_a, cos2
        s.rot_b, s.sin2, s.low_q, s.bz_sq, s.bz = rot_b, sin2, low_q, bz_sq, bz
        s.conv_sq, s.o_rstd, s.eps_o, s.g_taps, s.conv_taps = conv_sq, o_rstd, eps_o, g_taps, conv_taps
        s.qk_scaled, s.qk_gain, s.b_lo, s.k_lo, s.o_sb = qk_scaled, qk_gain, b_lo, k_lo, o_sb
        s.ratio, s.neg_lam, s.project, s.xT_hi, s.xT_lo = ratio, neg_lam, project, xT_hi, xT_lo
        s.ident, s.ident_b, s.causal_b, s.x_again, s.x_rows = ident, ident_b, causal_b, x_again, x_rows
        s.gain2, s.ffn_norm_gain, s.out_rows, s.h_sb, s.xn2_rows = gain2, ffn_norm_gain, out_rows, h_sb, xn2_rows
        s.hn, s.load_gate_up, s.load_down, s.w_route, s.w_group_router = hn, load_gate_up, load_down, w_route, w_group_router
        s.w_expert_router, s.rstd_c, s.h_rstd, s.h_ss, s.m_hi = w_expert_router, rstd_c, h_rstd, h_ss, m_hi
        s.wo_hi, s.h_sq, s.hnT, s.logitsT, s.logits = wo_hi, h_sq, hnT, logitsT, logits
        s.m_lo, s.wo_lo, s.ones_col, s.at, s.iota_e = m_lo, wo_lo, ones_col, at, iota_e
        s.iota_r, s.tok, s.weight, s.slot, s.own_e = iota_r, tok, weight, slot, own_e
        s.cnt, s.iota_b, s.full, s.ones_e, s.rows = cnt, iota_b, full, ones_e, rows
        s.hi_ready, s.w_lo, s.raw, s.w_hi, s.lo_ready = hi_ready, w_lo, raw, w_hi, lo_ready
        s.loaded, s.table_parts, s.table_summed, s.table, s.before_b = loaded, table_parts, table_summed, table, before_b
        s.ones_b, s.kept, s.spare_n, s.spare_e, s.idx_g = ones_b, kept, spare_n, spare_e, idx_g
        s.idx_s, s.y_sb, s.hidT_hi, s.rT_hi, s.silu = idx_s, y_sb, hidT_hi, rT_hi, silu
        s.hidT_lo, s.rT_lo, s.w_slot, s.hid, s.spare_xT = hidT_lo, rT_lo, w_slot, hid, spare_xT
        s.spare_hT = spare_hT
        heads(nc, sem, s)
        mix_out(nc, sem, s)
        route(nc, sem, s)
        experts(nc, sem, s)


def low_half(nc, dve, t, hi_ready, hi, lo, ps, ready):
    b = t % 2
    dve.wait_ge(hi_ready, t + 1)
    cols = slice(t * P, (t + 1) * P)
    dve.tensor_tensor(lo[:, :, cols].rearrange("p (a c) q -> p a c q", a=2),
                      ps[:, 2 * b:2 * b + 2, :].rearrange("p a (c q) -> p a c q", q=P),
                      hi[:, :, cols].bitcast(F32).rearrange("p (a c) q -> p a c q", a=2),
                      ALU.subtract).then_inc(ready, 1)


def product_T(pe, ps, bank, w_hi, w_lo, xT_hi, xT_lo):
    for half in range(2):
        cols = slice(half * 512, (half + 1) * 512)
        for c in range(KC):
            pe.matmul(ps[:, bank + half, :], w_hi[:, c, :], xT_hi[:, c, cols], start=(c == 0), stop=False)
            pe.matmul(ps[:, bank + half, :], w_hi[:, c, :], xT_lo[:, c, cols], start=False, stop=False)
            ins = pe.matmul(ps[:, bank + half, :], w_lo[:, c, :], xT_hi[:, c, cols], start=False,
                            stop=(c == KC - 1))
    return ins


def heads(nc, sem, s):
    ps = s.ps
    b_multiplied = sem("b_multiplied")
    bz_ready = sem("bz_ready")
    bz_used = sem("bz_used")
    qk_squared = sem("qk_squared")
    ss_ready = sem("ss_ready")
    qk_rstd_ready = sem("qk_rstd_ready")
    qk_read = sem("qk_read")
    v_copied = sem("v_copied")
    scaled_twice = sem("scaled_twice")
    rotated = sem("rotated")
    turned = sem("turned")
    stack_hi = sem("stack_hi")
    stack_ready = sem("stack_ready")
    scores = [sem(f"scores{m}") for m in range(2)]
    max_ready = [sem(f"max_ready{m}") for m in range(2)]
    exp_done = [sem(f"exp_done{m}") for m in range(2)]
    mixed = sem("mixed")
    maps_turned = sem("maps_turned")
    mapsT_copied = sem("mapsT_copied")
    pv_done = sem("pv_done")
    o_squared = sem("o_squared")
    o_rstd_ready = sem("o_rstd_ready")
    o_scaled = sem("o_scaled")
    o_turned = sem("o_turned")
    oT_copied = sem("oT_copied")
    dve_steps = sem("dve_steps_heads")
    pool_steps = sem("pool_steps_heads")
    act_steps = sem("act_steps_heads")

    def bank_cols(b, n):
        return ps[:, b:b + 2, :].rearrange("p a n -> p (a n)")[:, 0:n]

    def another(eng, h):
        return eng.If(h < HEADS - 1)

    def score_cols(m, n):
        return bank_cols(2 + 2 * m, n)

    with nc.Block() as block:
        @block.sync
        def _(sp):
            with sp.Fori(0, HEADS - 1) as h:
                sp.wait_ge(s.q_lo_ready, h * PIECES + PIECES)
                s.load_q(sp, h + 1)
                sp.wait_ge(s.b_lo_ready, h + 1)
                s.load_b(sp, h + 1)
            sp.wait_ge(b_multiplied, HEADS + 1)
            for n in range(2):
                half = slice(n * KC // 2, (n + 1) * KC // 2)
                sp.dma_start(s.wo_raw[:, half, :], s.w_out[0].rearrange("(k p) n -> p k n", p=P)[:, half, :]).then_inc(s.wo_in, 16)

        @block.scalar
        def _(act):
            own = Order(act, act_steps)
            with act.Fori(0, HEADS) as h:
                own.enter(h, NT)
                for i in range(NT + 1):
                    if i < NT:
                        b = i % 2
                        act.wait_ge(s.projected, h * NT + (i + 2))
                        act.wait_ge(ss_ready, h * NT + (i + 1))
                        act.activation(s.qk_sq[:], ps[:, 2 + i % 4, 0:256].rearrange("p (g d) -> p g d", g=4),
                                       ACT.Square, scale=DK ** -0.5).then_inc(qk_squared, 1)
                        act.copy(s.v_sb[:, i, :], ps[:, 2 + i % 4, 256:384]).then_inc(v_copied, 1)
                    if i == 1:
                        act.wait_ge(s.b_in, h * 16 + 16)
                        act.wait_ge(bz_used, h * 2 + 2)
                        act.copy(s.b_hi[:], s.b_raw[:]).then_inc(s.b_hi_ready, 1)
                    if i >= 1:
                        b, cols = (i - 1) % 2, slice((i - 1) * P, i * P)
                        act.wait_ge(turned, h * NT + i)
                        act.copy(s.q_stack[:, :, cols], ps[:, 6 + b, 0:256].rearrange("p (m q) -> p m q", m=2)).then_inc(stack_hi, 1)
                        act.copy(s.k_hi[:, :, cols], ps[:, 6 + b, 256:512].rearrange("p (m q) -> p m q", m=2)).then_inc(stack_hi, 1)
                for step in range(NT + 4):
                    t = step - 2
                    if 0 <= t < NT:
                        act.wait_ge(maps_turned, h * NT + (t + 1))
                        if t >= 2:
                            act.wait_ge(pv_done, h * NT + (t - 1))
                        act.copy(s.mapsT[t % 2][:, 0:t + 1, :], bank_cols(6, (t + 1) * P).rearrange("p (k q) -> p k q", q=P)).then_inc(mapsT_copied, 1)
                    if step < NT:
                        n = (step + 1) * P
                        for m in range(2):
                            act.wait_ge(max_ready[m], h * NT + (step + 1))
                            if step >= 2 and m == 0:
                                act.wait_ge(maps_turned, h * NT + (step - 1))
                            act.activation(s.probs[step % 2][:, m, 0:n], score_cols(m, n), ACT.Exp,
                                           bias=s.neg_max[:, step % 2, m:m + 1],
                                           accum_out=s.sums[:, step, m:m + 1]).then_inc(exp_done[m], 1)
                    if 1 <= step <= PIECES:
                        with another(act, h):
                            act.wait_ge(s.q_in, h * 48 + 96)
                            act.wait_ge(s.projected, h * NT + (NT + 1))
                            s.round_q(act, step - 1)
                    t = step - 3
                    if 0 <= t < NT:
                        act.wait_ge(pv_done, h * NT + (t + 1))
                        if t >= 1:
                            own.wait(t)
                        own.mark(act.activation(s.o_sq[:], ps[:, 0, 0:DV], ACT.Square, scale=s.inv_sums[:, t, 0:1],
                                                accum_out=s.o_ss[:, t % 2:t % 2 + 1]))
                        own.wait(t + 1)
                        act.sem_inc(o_squared, 1)
                    t = step - 4
                    if 0 <= t < NT:
                        act.wait_ge(o_turned, h * NT + (t + 1))
                        act.activation(s.mixT[:, bass.ds(h, 1), t * P:(t + 1) * P].rearrange("p a q -> p (a q)"),
                                       ps[:, 1, 0:P], ACT.Identity, scale=s.sub_gain[:]).then_inc(oT_copied, 1)
                own.leave(HEADS)

        @block.gpsimd
        def _(pool):
            own = Order(pool, pool_steps)
            with pool.Fori(0, HEADS) as h:
                own.enter(h, 2 + NT * 4 + NT)
                for i in range(NT):
                    b = i % 2
                    pool.wait_ge(ss_ready, h * NT + (i + 2))
                    own.then(pool.tensor_tensor(s.qk_rstd[:, b, :], s.qk_ss[:, b, :], s.eps_qk[:, 0:4], ALU.add))
                    pool.tensor_tensor(s.qk_rstd[:, b, :], s.qk_rstd[:, b, :], s.neg_half[:, 0:4], ALU.pow).then_inc(qk_rstd_ready, 1)
                    pool.wait_ge(scaled_twice, h * NT + (i + 1))
                    twice = s.qk_twice[b]
                    half = ROT // 2
                    own.mark(pool.tensor_tensor(s.rot_a[:], twice[:, :, 0, 0:ROT],
                                                s.cos2[:, i:i + 1, :].to_broadcast([P, 4, ROT]), ALU.mult))
                    own.mark(pool.tensor_tensor(s.rot_b[:, :, 0:half], twice[:, :, 0, half:ROT],
                                                s.sin2[:, i:i + 1, 0:half].to_broadcast([P, 4, half]), ALU.mult))
                    own.then(pool.tensor_tensor(s.rot_b[:, :, half:ROT], twice[:, :, 0, 0:half],
                                                s.sin2[:, i:i + 1, half:ROT].to_broadcast([P, 4, half]), ALU.mult))
                    pool.tensor_tensor(twice[:, :, :, 0:ROT], s.rot_a[:].unsqueeze(2).to_broadcast([P, 4, 2, ROT]),
                                       s.rot_b[:].unsqueeze(2).to_broadcast([P, 4, 2, ROT]), ALU.add).then_inc(rotated, 1)
                    pool.wait_ge(rotated, h * NT + (i + 1))
                for t in range(NT):
                    if 1 <= t <= PIECES:
                        with another(pool, h):
                            s.low_q(pool, t - 1, h * PIECES + (PIECES + t))
                    if t == PIECES + 1:
                        pool.wait_ge(bz_ready, h + 1)
                        own.then(pool.tensor_tensor(s.bz_sq[:], s.bz[:], s.bz[:], ALU.mult))
                    if t == PIECES + 2:
                        own.then(pool.tensor_tensor(s.conv_sq[:], s.conv_sq[:], s.bz_sq[:], ALU.add))
                        pool.sem_inc(bz_used, 1)
                    c = slice(t % 2, t % 2 + 1)
                    pool.wait_ge(o_squared, h * NT + (t + 1))
                    own.then(pool.tensor_tensor(s.o_rstd[:, c], s.o_ss[:, c], s.eps_o[:], ALU.add))
                    pool.tensor_tensor(s.o_rstd[:, c], s.o_rstd[:, c], s.neg_half[:, 0:1], ALU.pow).then_inc(o_rstd_ready, 1)
                own.leave(HEADS)

        @block.vector
        def _(dve):
            own = Order(dve, dve_steps)
            dve.sem_inc(ss_ready, 1)
            dve.sem_inc(bz_used, 2)
            dve.sem_inc(o_scaled, 1)
            with dve.Fori(0, HEADS) as h:
                own.enter(h, 2 + NT + 2 * NT)
                z = s.mixT[:, bass.ds(h + HEADS, 1), :].rearrange("p c t -> p (c t)")
                own.mark(dve.tensor_copy(s.g_taps[:], s.conv_taps[:, bass.ds(h, 1), :].rearrange("p m j -> p (m j)")))
                for i in range(NT + 1):
                    if i < NT:
                        b = i % 2
                        dve.wait_ge(qk_squared, h * NT + (i + 1))
                        dve.reduce_sum(s.qk_ss[:, b, :], s.qk_sq[:], axis=AX.X).then_inc(ss_ready, 1)
                        dve.wait_ge(qk_rstd_ready, h * NT + (i + 1))
                        dve.wait_ge(v_copied, h * NT + (i + 1))
                        dve.tensor_tensor(s.qk_scaled[0][:], ps[:, 2 + i % 4, 0:256].rearrange("p (g d) -> p g d", g=4),
                                          s.qk_rstd[:, b, :].unsqueeze(2).to_broadcast([P, 4, DK]), ALU.mult).then_inc(qk_read, 1)
                        dve.wait_ge(qk_read, h * NT + (i + 1))
                        if i >= 2:
                            dve.wait_ge(turned, h * NT + (i - 1))
                        own.mark(dve.tensor_tensor(s.qk_twice[b][:], s.qk_scaled[0][:].unsqueeze(2).to_broadcast([P, 4, 2, DK]),
                                                   s.qk_gain[:].rearrange("p a m d -> p (a m) d").unsqueeze(2).to_broadcast([P, 4, 2, DK]),
                                                   ALU.mult))
                        own.wait(own.n)
                        dve.sem_inc(scaled_twice, 1)
                    if i == 2:
                        dve.wait_ge(s.b_hi_ready, h + 1)
                        dve.tensor_tensor(s.b_lo[:], s.b_raw[:], s.b_hi[:].bitcast(F32), ALU.subtract).then_inc(s.b_lo_ready, 1)
                    if i == NT:
                        dve.wait_ge(b_multiplied, h + 2)
                        dve.tensor_tensor(s.bz[:].rearrange("p (a n) -> p a n", a=2), ps[:, 0:2, :],
                                          z.rearrange("p (a n) -> p a n", a=2), ALU.mult).then_inc(bz_ready, 1)
                    if i >= 1:
                        t = i - 1
                        b, cols = t % 2, slice(t * P, i * P)
                        dve.wait_ge(stack_hi, h * (2 * NT) + (2 * t + 2))
                        dve.tensor_tensor(s.q_stack[DK:, :, cols], ps[DK:, 6 + b, 0:256].rearrange("p (m q) -> p m q", m=2),
                                          s.q_stack[DK:, :, cols].bitcast(F32), ALU.subtract).then_inc(stack_ready, 1)
                        dve.tensor_tensor(s.k_lo[:, :, cols], ps[:, 6 + b, 256:512].rearrange("p (m q) -> p m q", m=2),
                                          s.k_hi[:, :, cols].bitcast(F32), ALU.subtract).then_inc(stack_ready, 1)
                for step in range(NT + 4):
                    for m in range(2):
                        if step < NT:
                            dve.wait_ge(scores[m], h * NT + (step + 1))
                            dve.tensor_reduce(s.neg_max[:, step % 2, m:m + 1], score_cols(m, (step + 1) * P), axis=AX.X,
                                              op=ALU.max, negate=True).then_inc(max_ready[m], 1)
                        t = step - 4
                        if m == 1 and 0 <= t < NT:
                            dve.wait_ge(o_rstd_ready, h * NT + (t + 1))
                            if t >= 2:
                                dve.wait_ge(o_turned, h * NT + (t - 1))
                            dve.tensor_scalar(s.o_sb[t % 2][:], ps[:, 0, 0:DV], s.inv_sums[:, t, 0:1], s.o_rstd[:, t % 2:t % 2 + 1],
                                              ALU.mult, ALU.mult).then_inc(o_scaled, 1)
                    if step == 1:
                        dve.wait_ge(bz_ready, h + 1)
                        own.wait(1)
                        own.then(dve.tensor_scalar(z, s.bz[:], s.g_taps[:, 3:4], None, ALU.mult))
                        dve.sem_inc(bz_used, 1)
                    t = step - 1
                    if 0 <= t < NT:
                        n = (t + 1) * P
                        for m in range(2):
                            dve.wait_ge(exp_done[m], h * NT + (t + 2))
                        own.then(dve.reciprocal(s.inv_sums[:, t, :], s.sums[:, t, :]))
                        own.then(dve.tensor_scalar(s.ratio[:, 0:1], s.inv_sums[:, t, 1:2], s.sums[:, t, 0:1], s.neg_lam[:],
                                                   ALU.mult, ALU.mult))
                        dve.scalar_tensor_tensor(s.probs[t % 2][:, 0, 0:n], s.probs[t % 2][:, 1, 0:n], s.ratio[:, 0:1],
                                                 s.probs[t % 2][:, 0, 0:n], ALU.mult, ALU.add).then_inc(mixed, 1)
                own.leave(HEADS)

        @block.tensor
        def _(pe):
            for primed in (b_multiplied, exp_done[0], exp_done[1], oT_copied):
                pe.sem_inc(primed, 1)

            with pe.Fori(0, HEADS) as h:
                for i in range(2, NT + 2):
                    if i < NT:
                        if i == 2:
                            pe.wait_ge(exp_done[1], h * NT + 1)
                        if i >= 4:
                            pe.wait_ge(qk_read, h * NT + (i - 3))
                            pe.wait_ge(v_copied, h * NT + (i - 3))
                        s.project(pe, h, i)
                    if i == NT:
                        pe.wait_ge(s.b_lo_ready, h + 1)
                        pe.wait_ge(o_scaled, h * NT + 1)
                        pe.wait_ge(oT_copied, h * NT + 1)
                        product_T(pe, ps, 0, s.b_hi, s.b_lo, s.xT_hi, s.xT_lo).then_inc(b_multiplied, 1)
                    t = i - 2
                    pe.wait_ge(rotated, h * NT + (t + 1))
                    if t >= 2:
                        pe.wait_ge(stack_ready, h * (2 * NT) + 2 * (t - 1))
                    for g in range(4):
                        ins = pe.transpose(ps[:, 6 + t % 2, g * P:(g + 1) * P],
                                           s.qk_twice[t % 2][:, g, :, :].rearrange("p e d -> p (e d)"), s.ident[:])
                    ins.then_inc(turned, 1)
                for step in range(NT + 4):
                    if step < NT:
                        if step == 0:
                            pe.wait_ge(stack_ready, h * (2 * NT) + 2 * NT)
                            pe.wait_ge(v_copied, h * NT + NT)
                        n = (step + 1) * P
                        for m in range(2):
                            pe.wait_ge(exp_done[m], h * NT + (step + 1))
                            q = s.q_stack[:, m, step * P:n]
                            for k0 in range(0, n, 512):
                                k1 = min(k0 + 512, n)
                                o = score_cols(m, 1024)[:, k0:k1]
                                pe.matmul(o, q, s.k_hi[:, m, k0:k1], start=True, stop=False)
                                if k1 == n:
                                    pe.matmul(o[:, k1 - k0 - P:], s.ident_b[:], s.causal_b[:], start=False,
                                              stop=False, skip_group_check=True)
                                ins = pe.matmul(o, q, s.k_lo[:, m, k0:k1], start=False, stop=True)
                            ins.then_inc(scores[m], 1)
                    t = step - 2
                    if 0 <= t < NT:
                        pe.wait_ge(mixed, h * NT + (t + 1))
                        if t >= 1:
                            pe.wait_ge(mapsT_copied, h * NT + t)
                        for k in range(t + 1):
                            ins = pe.transpose(ps[:, 6 + k // 4, (k % 4) * P:(k % 4 + 1) * P],
                                               s.probs[t % 2][:, 0, k * P:(k + 1) * P], s.ident[:])
                        ins.then_inc(maps_turned, 1)
                    t = step - 3
                    if 0 <= t < NT:
                        pe.wait_ge(mapsT_copied, h * NT + (t + 1))
                        if t == 0:
                            pe.wait_ge(bz_ready, h + 1)
                        pe.wait_ge(o_scaled, h * NT + (t + 1))
                        for k in range(t + 1):
                            ins = pe.matmul(ps[:, 0, 0:DV], s.mapsT[t % 2][:, k, :], s.v_sb[:, k, :],
                                            start=(k == 0), stop=(k == t))
                        ins.then_inc(pv_done, 1)
                    t = step - 4
                    if 0 <= t < NT:
                        pe.wait_ge(o_scaled, h * NT + (t + 2))
                        pe.wait_ge(oT_copied, h * NT + (t + 1))
                        pe.transpose(ps[:, 1, 0:P], s.o_sb[t % 2][:], s.ident[:]).then_inc(o_turned, 1)
                    if NT <= step < NT + 2:
                        with another(pe, h):
                            if step == NT:
                                pe.wait_ge(s.q_lo_ready, h * PIECES + 2 * PIECES)
                                pe.wait_ge(exp_done[0], h * NT + (NT + 1))
                            s.project(pe, h + 1, step - NT)
            pe.nop()
def mix_out(nc, sem, s):
    ps = s.ps
    xa_in = [sem(f"xa_in{b}") for b in range(2)]
    gain2_in = sem("gain2_in")
    route_in = sem("route_in")
    wo_hi_ready = sem("wo_hi_ready")
    wo_lo_ready = sem("wo_lo_ready")
    conv_summed = sem("conv_summed")
    conv_mean = sem("conv_mean")
    conv_rstd = sem("conv_rstd")
    m_hi_ready = sem("m_hi_ready")
    m_lo_ready = sem("m_lo_ready")
    product_done = sem("product_done")
    part_added = sem("part_added")
    h_ready = sem("h_ready")
    h_squared = sem("h_squared")
    h_rstd_ready = sem("h_rstd_ready")
    hn_ready = sem("hn_ready")
    hn_turned = sem("hn_turned")
    hnT_copied = sem("hnT_copied")
    routed = sem("routed")
    logits_copied = sem("logits_copied")
    h_stored = sem("h_stored")
    hn_stored = sem("hn_stored")
    stored = sem("stored")
    pool_steps = sem("pool_steps_mix")

    def turns(eng, turn):
        with eng.Fori(0, (NT - 2) // 2) as j:
            for b in range(2):
                turn(j * 2 + b, j + b, b, True)
        turn(NT - 2, (NT - 1) // 2, 0, True)
        turn(NT - 1, None, 1, False)

    with nc.Block() as block:
        @block.sync
        def _(sp):
            sp.sem_inc(stored, 1)
            for k in range(2):
                sp.dma_start(s.x_again[k][:], s.x_rows[k * P:(k + 1) * P, :]).then_inc(xa_in[k], 16)
            sp.dma_start(s.gain2[:], s.ffn_norm_gain[0:1, :].to_broadcast([P, D])).then_inc(gain2_in, 16)

            def turn(t, half, b, more):
                sp.wait_ge(h_ready, t + 1)
                sp.dma_start(s.out_rows[bass.ds(t * P, P), :], s.h_sb[b][:]).then_inc(h_stored, 16)
                sp.wait_ge(hn_ready, t + 1)
                sp.dma_start(s.xn2_rows[bass.ds(t * P, P), :], s.hn[b][:].rearrange("p c q -> p (c q)")).then_inc(hn_stored, 16)
                if not isinstance(t, int):
                    sp.dma_start(s.x_again[b][:], s.x_rows[bass.ds(t * P + 2 * P, P), :]).then_inc(xa_in[b], 16)
                sp.wait_ge(h_stored, t * 16 + 16)
                sp.wait_ge(hn_stored, t * 16 + 16)
                sp.sem_inc(stored, 1)

            with sp.Fori(0, (NT - 2) // 2) as j:
                for b in range(2):
                    turn(j * 2 + b, j + b, b, True)
            sp.wait_ge(m_lo_ready, NT)
            for q in range(2, 4):
                s.load_gate_up(sp, 0, 0, q)
            for q in range(2):
                s.load_down(sp, 0, 0, q)
            turn(NT - 2, (NT - 1) // 2, 0, True)
            turn(NT - 1, None, 1, False)

        @block.gpsimd
        def _(pool):
            own = Order(pool, pool_steps)
            with nc.allow_non_contiguous_dma(reason="the routers' narrow weights"):
                pool.dma_start(s.w_route[:, :, 0:GROUPS], s.w_group_router[0].rearrange("(p c) g -> p c g", c=KC)).then_inc(route_in, 16)
                for g in range(GROUPS):
                    pool.dma_start(s.w_route[:, :, GROUPS + g * PER_GROUP:GROUPS + (g + 1) * PER_GROUP],
                                   s.w_expert_router[0, g].rearrange("(p c) e -> p c e", c=KC)).then_inc(route_in, 16)
            pool.wait_ge(conv_mean, 1)
            pool.tensor_tensor(s.rstd_c[:], s.rstd_c[:], s.neg_half[:], ALU.pow).then_inc(conv_rstd, 1)
            with pool.Fori(0, NT // 2) as j:
                own.enter(j, 2)
                for b in range(2):
                    pool.wait_ge(h_squared, j * 2 + (b + 2))
                    own.then(pool.tensor_tensor(s.h_rstd[:, b:b + 1], s.h_ss[:, b:b + 1], s.eps_qk[:, 0:1], ALU.add))
                    pool.tensor_tensor(s.h_rstd[:, b:b + 1], s.h_rstd[:, b:b + 1], s.neg_half[:, 0:1], ALU.pow).then_inc(h_rstd_ready, 1)
                own.leave(NT // 2)

        @block.scalar
        def _(act):
            def round_mix(t, b):
                act.copy(s.m_hi[b][:], s.mixT[:, :, bass.ds(t * P, P)]).then_inc(m_hi_ready, 1)

            round_mix(0, 0)
            act.wait_ge(s.wo_in, 32)
            for k in range(KC):
                act.copy(s.wo_hi[:, k, :], s.wo_raw[:, k, :]).then_inc(wo_hi_ready, 1)
            round_mix(1, 1)

            def turn(t, half, b, more):
                if not isinstance(t, int):
                    act.wait_ge(product_done, t * 2 + 2)
                    round_mix(t + 2, b)
                act.wait_ge(h_ready, t + 1)
                act.wait_ge(h_squared, t + 1)
                act.activation(s.h_sq[:], s.h_sb[b][:], ACT.Square, scale=D ** -0.5,
                               accum_out=s.h_ss[:, b:b + 1]).then_inc(h_squared, 1)
                act.wait_ge(hn_turned, t + 1)
                act.wait_ge(routed, t + 1)
                act.copy(s.hnT[:].rearrange("p (a c) q -> p a (c q)", a=2), ps[:, 4:6, :]).then_inc(hnT_copied, 1)
                act.wait_ge(routed, t + 2)
                act.copy(s.logitsT[:, bass.ds(t * P, P)], ps[0:GROUPS + E, 6, 0:P]).then_inc(logits_copied, 1)

            turns(act, turn)
            act.wait_ge(routed, NT + 2)
            act.copy(s.logits[:], ps[:, 6, 0:NT * (GROUPS + E)].rearrange("p (t g) -> p t g", t=NT)).then_inc(logits_copied, 1)

        @block.vector
        def _(dve):
            def low_mix(t, b):
                dve.wait_ge(m_hi_ready, t + 1)
                dve.tensor_tensor(s.m_lo[b][:], s.mixT[:, :, bass.ds(t * P, P)], s.m_hi[b][:].bitcast(F32),
                                  ALU.subtract).then_inc(m_lo_ready, 1)

            def add_parts(t, uses, b):
                dve.wait_ge(xa_in[b], uses * 16 + 16)
                dve.wait_ge(product_done, t * 2 + 1)
                banks = lambda n: ps[:, n:n + 2, :].rearrange("p a n -> p (a n)")
                dve.tensor_tensor(s.h_sb[b][:], banks(0), s.x_again[b][:], ALU.add).then_inc(part_added, 1)
                dve.wait_ge(part_added, t + 1)
                dve.wait_ge(product_done, t * 2 + 2)
                dve.scalar_tensor_tensor(s.h_sb[b][:], banks(2), s.rstd_c[:, bass.ds(t, 1)], s.h_sb[b][:],
                                         ALU.mult, ALU.add).then_inc(h_ready, 1)

            dve.sem_inc(h_squared, 1)
            low_mix(0, 0)
            for k in range(KC):
                dve.wait_ge(wo_hi_ready, k + 1)
                dve.tensor_tensor(s.wo_lo[:, k, :], s.wo_raw[:, k, :], s.wo_hi[:, k, :].bitcast(F32),
                                  ALU.subtract).then_inc(wo_lo_ready, 1)
            low_mix(1, 1)
            dve.wait_ge(conv_summed, 1)
            dve.tensor_scalar(s.rstd_c[:], ps[:, 7, 0:NT], 1.0 / CONV, EPS, ALU.mult, ALU.add).then_inc(conv_mean, 1)
            dve.wait_ge(conv_rstd, 1)
            dve.wait_ge(gain2_in, 16)
            add_parts(0, 0, 0)

            def turn(t, half, b, more):
                if not isinstance(t, int):
                    low_mix(t + 2, b)
                dve.wait_ge(h_rstd_ready, t + 1)
                rows = lambda a: a.rearrange("p (q c) -> p q c", c=KC)
                dve.scalar_tensor_tensor(s.hn[b][:].rearrange("p c q -> p q c"), rows(s.h_sb[b][:]), s.h_rstd[:, b:b + 1],
                                         rows(s.gain2[:]), ALU.mult, ALU.mult).then_inc(hn_ready, 1)
                if more:
                    dve.wait_ge(stored, t + 1)
                    add_parts(t + 1, half, 1 - b)

            turns(dve, turn)

        @block.tensor
        def _(pe):
            def part(t, b, n):
                for k in range(4 * n, 4 * n + 4):
                    first, last = k == 4 * n, k == 4 * n + 3
                    if isinstance(t, int) and t == 0:
                        pe.wait_ge(wo_lo_ready, k + 1)
                    for half in range(2):
                        o, cols = ps[:, 2 * n + half, :], slice(half * 512, (half + 1) * 512)
                        pe.matmul(o, s.m_hi[b][:, k, :], s.wo_hi[:, k, cols], start=first, stop=False)
                        pe.matmul(o, s.m_hi[b][:, k, :], s.wo_lo[:, k, cols], start=False, stop=False)
                        ins = pe.matmul(o, s.m_lo[b][:, k, :], s.wo_hi[:, k, cols], start=False, stop=last)
                ins.then_inc(product_done, 1)

            pe.sem_inc(hnT_copied, 1)
            pe.sem_inc(logits_copied, 1)
            pe.sem_inc(routed, 1)
            for t in range(NT):
                ins = pe.matmul(ps[:, 7, t:t + 1], s.conv_sq[:, t * P:(t + 1) * P], s.ones_col[:], start=True, stop=True)
            ins.then_inc(conv_summed, 1)
            pe.wait_ge(m_lo_ready, 1)
            part(0, 0, 0)
            part(0, 0, 1)
            pe.wait_ge(route_in, 16 * (1 + GROUPS))

            def turn(t, half, b, more):
                if more:
                    pe.wait_ge(m_lo_ready, t + 2)
                    pe.wait_ge(part_added, t + 1)
                    part(t + 1, 1 - b, 0)
                pe.wait_ge(hn_ready, t + 1)
                pe.wait_ge(hnT_copied, t + 1)
                for c in range(KC):
                    ins = pe.transpose(ps[:, 4 + c // 4, (c % 4) * P:(c % 4 + 1) * P], s.hn[b][:, c, :], s.ident[:])
                ins.then_inc(hn_turned, 1)
                if more:
                    pe.wait_ge(h_ready, t + 1)
                    part(t + 1, 1 - b, 1)
                pe.wait_ge(hnT_copied, t + 2)
                pe.wait_ge(logits_copied, t + 1)
                for c in range(KC):
                    ins = pe.matmul(ps[0:GROUPS + E, 6, 0:P], s.w_route[:, c, :], s.hnT[:, c, :], start=(c == 0), stop=(c == KC - 1))
                ins.then_inc(routed, 1)

            turns(pe, turn)
            pe.wait_ge(logits_copied, NT + 1)
            n = GROUPS + E
            for t in range(NT):
                ins = pe.transpose(ps[:, 6, t * n:(t + 1) * n], s.logitsT[:, t * P:(t + 1) * P], s.ident[0:n, 0:n])
            ins.then_inc(routed, 1)




def place(at, rooms, name, shape, dtype=F32):
    n = 1
    for d in shape[1:]:
        n *= d
    size = -(-n * (2 if dtype == BF16 else 4) // 32) / 32
    room = [r for r in rooms if r[0] + size <= r[1]][0]
    room[0] += size
    return at(name, room[0] - size, shape, dtype)


def route(nc, sem, s):
    ps = s.ps
    iotas = sem("iotas")
    shifted = sem("shifted")
    group_exp = sem("group_exp")
    top_diff = sem("top_diff")
    top_exp = sem("top_exp")
    chosen = sem("chosen")
    counted = sem("counted")
    dve_steps = sem("dve_steps_route")
    L = s.logits
    rooms = [[160.0, 166.0], [168.5, 194.0], [195.0, 201.0]]

    def tile(name, shape, dtype=F32):
        return place(s.at, rooms, name, shape, dtype)

    gl = tile("gl", [P, NT, GROUPS])
    gtmp = tile("gtmp", [P, NT, GROUPS])
    gmask = tile("gmask", [P, NT, GROUPS])
    stat = [tile(f"stat{j}", [P, NT]) for j in range(7)]
    el = tile("el", [P, NT, E])
    tmp = tile("tmp", [P, NT, E])
    hot = [tile(f"hot{k}", [P, NT, E]) for k in range(TOP_K)]
    mask = tile("mask", [P, NT, E], BF16)
    pos = tile("pos", [P, NT, E])
    in_slot = tile("in_slot", [P, TOP_K * NT, SLOTS])
    entry = tile("entry", [P, TOP_K * NT, 2, E])
    table_f = tile("table_f", [SLOTS, 2, E])
    iota_e, iota_r, tok, weight, slot, own_e, cnt = s.iota_e, s.iota_r, s.tok, s.weight, s.slot, s.own_e, s.cnt

    with nc.Block() as block:
        @block.sync
        def _(sp):
            for q in range(2):
                s.load_gate_up(sp, 0, 0, q)
            for q in range(4):
                s.load_gate_up(sp, 1, 1, q)
            for q in range(2):
                s.load_down(sp, 1, 1, q)

        @block.gpsimd
        def _(pool):
            def iota(out, pattern, base, per_partition=0):
                pool.iota(out, pattern=pattern, base=base, channel_multiplier=per_partition,
                          allow_small_or_imprecise_dtypes=True).then_inc(iotas, 1)

            iota(iota_e[:], [[1, E]], 0)
            iota(tok[:], [[P, NT]], -NO_TOKEN, 1)
            iota(iota_r[:], [[1, SLOTS]], 0)
            iota(s.iota_b[:], [[1, SPARE]], 0)
            iota(s.full[:], [[SLOTS, MORE]], SLOTS)
            pool.memset(s.ones_e[:], 1.0).then_inc(iotas, 1)
            for b in range(2):
                pool.memset(s.rows[b][:], 0.0).then_inc(iotas, 1)
            for k in (2, 3, 0):
                pool.wait_ge(s.hi_ready[k], 1)
                pool.tensor_tensor(s.w_lo[0][k][:], s.raw[0][k][:], s.w_hi[k][:].bitcast(F32),
                                   ALU.subtract).then_inc(s.lo_ready[k], 1)

        @block.scalar
        def _(act):
            def split_hi(k):
                act.wait_ge(s.loaded[0][k], 32 if k < 4 else 16)
                act.copy(s.w_hi[k][:], s.raw[0][k][:]).then_inc(s.hi_ready[k], 1)

            split_hi(2)
            act.wait_ge(shifted, 1)
            act.activation(gl[:], gl[:], ACT.Exp).then_inc(group_exp, 1)
            act.wait_ge(top_diff, 1)
            act.activation(stat[5][:], stat[5][:], ACT.Exp).then_inc(top_exp, 1)
            for k in (3, 0, 1, 4, 5):
                split_hi(k)

        @block.vector
        def _(dve):
            own = Order(dve, dve_steps)
            do = own.then
            wide = lambda a, n: a.unsqueeze(2).to_broadcast([P, NT, n])
            row = lambda a, n, m: a.unsqueeze(1).to_broadcast([P, n, m])
            mul, add, sub, ge, gt, eq = ALU.mult, ALU.add, ALU.subtract, ALU.is_ge, ALU.is_gt, ALU.is_equal

            def lowest(out, values, top, n, scratch, low):
                do(dve.tensor_tensor(scratch, values, wide(top, n), ge))
                do(dve.scalar_tensor_tensor(scratch, scratch, -100.0, row(iota_e[:, 0:n], NT, n), mul, add))
                do(dve.tensor_reduce(low, scratch, axis=AX.X, op=ALU.min))
                do(dve.tensor_tensor(out, scratch, wide(low, n), eq))

            dve.wait_ge(iotas, 3)
            gmax, low, v1, gsum, v2, diff, total = (a[:] for a in stat[:7])
            gates = L[:, :, 0:GROUPS]
            do(dve.tensor_reduce(gmax, gates, axis=AX.X, op=ALU.max))
            dve.tensor_tensor(gl[:], gates, wide(gmax, GROUPS), sub).then_inc(shifted, 1)
            lowest(gmask[:], gates, gmax, GROUPS, gtmp[:], low)
            do(dve.tensor_scalar(gtmp[:], gmask[:], -MASKED, MASKED, mul, add))
            by_group = lambda a: a.rearrange("p t (g e) -> p t g e", g=GROUPS)
            of_group = lambda a: a.unsqueeze(3).to_broadcast([P, NT, GROUPS, PER_GROUP])
            do(dve.tensor_tensor(by_group(el[:]), by_group(L[:, :, GROUPS:]), of_group(gmask[:]), mul))
            do(dve.tensor_tensor(by_group(el[:]), by_group(el[:]), of_group(gtmp[:]), add))
            do(dve.tensor_reduce(v1, el[:], axis=AX.X, op=ALU.max))
            lowest(hot[0][:], el[:], v1, E, tmp[:], low)
            do(dve.scalar_tensor_tensor(el[:], hot[0][:], 2 * MASKED, el[:], mul, add))
            do(dve.tensor_reduce(v2, el[:], axis=AX.X, op=ALU.max))
            dve.tensor_tensor(diff, v2, v1, sub).then_inc(top_diff, 1)
            lowest(hot[1][:], el[:], v2, E, tmp[:], low)
            dve.tensor_tensor(mask[:], hot[0][:], hot[1][:], add).then_inc(chosen, 1)
            dve.wait_ge(group_exp, 1)
            do(dve.reduce_sum(gsum, gl[:], axis=AX.X))
            dve.wait_ge(top_exp, 1)
            do(dve.tensor_scalar(total, diff, 1.0, None, add))
            do(dve.tensor_tensor(total, total, gsum, mul))
            do(dve.reciprocal(weight[:, 0, :], total))
            do(dve.tensor_tensor(weight[:, 1, :], weight[:, 0, :], diff, mul))
            for k in range(TOP_K):
                part = slice(k * NT, (k + 1) * NT)
                do(dve.tensor_tensor(entry[:, part, 0, :], hot[k][:], wide(tok[:], E), mul))
                do(dve.tensor_tensor(entry[:, part, 1, :], hot[k][:], wide(weight[:, k, :], E), mul))
            dve.wait_ge(counted, 1)
            for k in range(TOP_K):
                do(dve.tensor_tensor(pos[:], hot[k][:], ps[:, 0, 0:NT * E].rearrange("p (t e) -> p t e", e=E), mul))
                do(dve.reduce_sum(slot[:, k, :], pos[:], axis=AX.X))
            do(dve.tensor_tensor(in_slot[:], slot[:].rearrange("p k t -> p (k t)").unsqueeze(2).to_broadcast([P, TOP_K * NT, SLOTS]),
                                 row(iota_r[:], TOP_K * NT, SLOTS), eq))
            dve.sem_inc(s.table_parts, 1)
            for k in range(TOP_K):
                do(dve.tensor_tensor(tmp[:], hot[k][:], row(iota_e[:], NT, E), mul))
                do(dve.reduce_sum(own_e[:, k, :], tmp[:], axis=AX.X))
            do(dve.tensor_copy(cnt[:], ps[:, 1, 0:E]))
            dve.wait_ge(s.table_summed, 1)
            do(dve.tensor_copy(table_f[:], ps[0:SLOTS, 2, 0:2 * E].rearrange("p (a b) -> p a b", a=2)))
            do(dve.tensor_scalar(s.table[:, 0:E, 0], table_f[:, 0, :], float(NO_TOKEN), None, add))
            do(dve.tensor_copy(s.table[:, 0:E, 1].bitcast(F32), table_f[:, 1, :]))

        @block.tensor
        def _(pe):
            pe.wait_ge(chosen, 1)
            for t in range(NT):
                for b in range(t + 1):
                    pe.matmul(ps[:, 0, t * E:(t + 1) * E], s.before_b[:] if b == t else s.ones_b[:], mask[:, b, :],
                              start=(b == 0), stop=(b == t))
            for t in range(NT):
                ins = pe.matmul(ps[:, 1, 0:E], s.ones_b[:], mask[:, t, :], start=(t == 0), stop=(t == NT - 1))
            ins.then_inc(counted, 1)
            pe.wait_ge(s.table_parts, 1)
            n = TOP_K * NT
            for j in range(n):
                ins = pe.matmul(ps[0:SLOTS, 2, 0:2 * E], in_slot[:, j, :], entry[:, j, :, :].rearrange("p a b -> p (a b)"),
                                start=(j == 0), stop=(j == n - 1))
            ins.then_inc(s.table_summed, 1)


def spare_rooms(s):
    rooms = [[s.kept[0][0], s.kept[0][1]], [186.0, 194.0], [195.0, 201.0]]
    x = Shared()
    x.over = place(s.at, rooms, "over", [P, E, MORE])
    x.extra = place(s.at, rooms, "extra", [P, E])
    x.ends = place(s.at, rooms, "ends", [P, E])
    x.starts = place(s.at, rooms, "starts", [P, E])
    x.passed = place(s.at, rooms, "passed", [P, SPARE, E])
    x.spare_f = place(s.at, rooms, "spare_f", [P, SPARE])
    x.which = place(s.at, rooms, "which", [P, TOP_K * NT, E])
    x.first = place(s.at, rooms, "first", [P, TOP_K * NT])
    x.nth = place(s.at, rooms, "nth", [P, TOP_K * NT])
    x.later = place(s.at, rooms, "later", [P, TOP_K * NT])
    x.beyond = place(s.at, rooms, "beyond", [P, TOP_K * NT, MORE])
    x.in_slot = place(s.at, rooms, "in_slot_s", [P, TOP_K * NT, SLOTS])
    x.in_block = place(s.at, rooms, "in_block", [P, TOP_K * NT, SPARE])
    x.entry = place(s.at, rooms, "entry_s", [P, TOP_K * NT, 2, SPARE])
    x.table_f = place(s.at, rooms, "table_s", [SLOTS, 2, SPARE])
    return x


def spare_places(dve, do, s, x):
    mul, add, sub = ALU.mult, ALU.add, ALU.subtract
    row = lambda a, k, m: a.unsqueeze(1).to_broadcast([P, k, m])
    col = lambda a, k, m: a.unsqueeze(2).to_broadcast([P, k, m])
    do(dve.tensor_tensor(x.over[:], col(s.cnt[:], E, MORE), row(s.full[:], E, MORE), ALU.is_gt))
    do(dve.reduce_sum(x.extra[:], x.over[:], axis=AX.X))
    do(dve.tensor_tensor_scan(x.ends[:], s.ones_e[:], x.extra[:], 0.0, mul, add))
    do(dve.tensor_tensor(x.starts[:], x.ends[:], x.extra[:], sub))
    do(dve.tensor_copy(s.spare_n[:], x.ends[:, E - 1:E]))
    do(dve.tensor_tensor(x.passed[:], row(x.ends[:], SPARE, E), col(s.iota_b[:], SPARE, E), ALU.is_le))
    do(dve.reduce_sum(x.spare_f[:], x.passed[:], axis=AX.X))
    do(dve.tensor_scalar(s.spare_e[:], x.spare_f[:], E - 1.0, None, ALU.min))


def spare_choices(dve, do, s, x):
    n = TOP_K * NT
    mul, add = ALU.mult, ALU.add
    flat = lambda a: a.rearrange("p k t -> p (k t)")
    row = lambda a, k, m: a.unsqueeze(1).to_broadcast([P, k, m])
    col = lambda a, k, m: a.unsqueeze(2).to_broadcast([P, k, m])
    do(dve.tensor_tensor(x.which[:], col(flat(s.own_e[:]), n, E), row(s.iota_e[:], n, E), ALU.is_equal))
    do(dve.tensor_tensor(x.which[:], x.which[:], row(x.starts[:], n, E), mul))
    do(dve.reduce_sum(x.first[:], x.which[:], axis=AX.X))
    do(dve.tensor_tensor(x.beyond[:], col(flat(s.slot[:]), n, MORE), row(s.full[:], n, MORE), ALU.is_ge))
    do(dve.reduce_sum(x.nth[:], x.beyond[:], axis=AX.X))
    do(dve.scalar_tensor_tensor(flat(s.slot[:]), x.nth[:], -float(SLOTS), flat(s.slot[:]), mul, add))
    do(dve.tensor_scalar(x.later[:], x.nth[:], 1.0, None, ALU.min))
    do(dve.tensor_tensor(x.first[:], x.first[:], x.nth[:], add))
    do(dve.tensor_tensor(x.first[:], x.first[:], x.later[:], mul))
    do(dve.tensor_scalar(x.first[:], x.first[:], -1.0, None, add))


def spare_parts(dve, do, s, x):
    n = TOP_K * NT
    eq, mul = ALU.is_equal, ALU.mult
    flat = lambda a: a.rearrange("p k t -> p (k t)")
    col = lambda a, k, m: a.unsqueeze(2).to_broadcast([P, k, m])
    do(dve.tensor_tensor(x.in_slot[:], col(flat(s.slot[:]), n, SLOTS), s.iota_r[:].unsqueeze(1).to_broadcast([P, n, SLOTS]), eq))
    do(dve.tensor_tensor(x.in_block[:], col(x.first[:], n, SPARE), s.iota_b[:].unsqueeze(1).to_broadcast([P, n, SPARE]), eq))
    for k in range(TOP_K):
        part = slice(k * NT, (k + 1) * NT)
        do(dve.tensor_tensor(x.entry[:, part, 0, :], x.in_block[:, part, :], col(s.tok[:], NT, SPARE), mul))
    do(dve.tensor_tensor(x.entry[:, :, 1, :], x.in_block[:], col(flat(s.weight[:]), n, SPARE), mul))


def spare_columns(dve, do, s, x):
    do(dve.tensor_copy(x.table_f[:], s.ps[0:SLOTS, 7, 0:2 * SPARE].rearrange("p (a b) -> p a b", a=2)))
    do(dve.tensor_scalar(s.table[:, E:, 0], x.table_f[:, 0, :], float(NO_TOKEN), None, ALU.add))
    do(dve.tensor_copy(s.table[:, E:, 1].bitcast(F32), x.table_f[:, 1, :]))


def experts(nc, sem, s):
    ps = s.ps
    used = [sem(f"used{k}") for k in range(6)]
    rows_in = [sem(f"rows_in{b}") for b in range(2)]
    scattered = sem("scattered")
    waited = sem("waited")
    y_free = sem("y_free")
    gather_idx = sem("gather_idx")
    scatter_idx = sem("scatter_idx")
    rows_turned = sem("rows_turned")
    rT_hi_ready = sem("rT_hi_ready")
    rT_lo_ready = sem("rT_lo_ready")
    gated = sem("gated")
    silu_ready = sem("silu_ready")
    weight_ready = sem("weight_ready")
    hid_ready = sem("hid_ready")
    hid_turned = sem("hid_turned")
    hT_hi_ready = sem("hT_hi_ready")
    hT_lo_ready = sem("hT_lo_ready")
    down_done = sem("down_done")
    y_ready = [sem(f"y_ready{n}") for n in range(2)]
    spare_steps = sem("spare_steps")
    sp_tab = spare_rooms(s)

    def has(e):
        return not isinstance(e, int) or 0 <= e < E

    def after(eng, semaphore, e, step=1):
        if not isinstance(e, int) or e >= 0:
            eng.wait_ge(semaphore, (e + 1) * step)

    def turns(turn):
        def run(eng):
            for e in range(-2, 2):
                turn(e, e % 2, e // 2)
            with eng.Fori(0, (E - 4) // 2) as j:
                for b in range(2):
                    turn(j * 2 + (b + 2), b, j + 1)
            for e in range(E - 2, E + 2):
                turn(e, e % 2, e // 2)
        return run

    def rows_loaded(eng, e, b, h, k):
        if has(e + k):
            eng.wait_ge(rows_in[(b + k) % 2], (h + (b + k) // 2 + 1) * 16)

    def last_down(e, k):
        return isinstance(e, int) and e == E - 1 and k >= 4

    def hi_of(e, k):
        return s.w_hi[k - 4] if last_down(e, k) else s.w_hi[k]

    def split_hi(act, e, b, h, d, k):
        if has(e + d) and not (isinstance(e, int) and e + d == 0):
            act.wait_ge(s.loaded[(b + d) % 2][k], (h + (b + d) // 2 + 1) * (32 if k < 4 else 16))
            if last_down(e + d, k):
                act.wait_ge(used[k - 4], E)
            else:
                after(act, used[k], e + (d - 1))
            act.copy(hi_of(e + d, k)[:], s.raw[(b + d) % 2][k][:]).then_inc(s.hi_ready[k], 1)

    def split_lo(eng, e, b, d, k):
        if has(e + d) and not (isinstance(e, int) and e + d == 0 and k in (0, 2, 3)):
            after(eng, s.hi_ready[k], e + d)
            eng.tensor_tensor(s.w_lo[(b + d) % 2][k][:], s.raw[(b + d) % 2][k][:], hi_of(e + d, k)[:].bitcast(F32),
                              ALU.subtract).then_inc(s.lo_ready[k], 1)

    banks45 = ps[:, 4:6, :].rearrange("p a (c q) -> p a c q", q=P)[:, :, :, 0:SLOTS]
    as_banks = lambda a: a.rearrange("p (a c) q -> p a c q", a=2)

    with nc.Block() as block:
        @block.sync
        def _(sp):
            def turn(e, b, h):
                for q in range(4):
                    after(sp, used[q], e - 1)
                    s.load_gate_up(sp, e + 1, 1 - b, q)
                for q in range(2):
                    after(sp, used[4 + q], e - 2)
                    s.load_down(sp, e, b, q)

            for q in range(4):
                sp.wait_ge(used[q], 1)
                s.load_gate_up(sp, 2, 0, q)
            with sp.Fori(0, (E - 4) // 2) as j:
                for b in range(2):
                    turn(j * 2 + (b + 2), b, None)
            turn(E - 2, 0, None)
            for q in range(2):
                after(sp, used[4 + q], E - 3)
                s.load_down(sp, E - 1, 1, q)

        @block.gpsimd
        def _(pool):
            last_row = pool.to_reg(T - 1)
            pool.sem_inc(y_free, 2)

            def turn(e, b, h):
                if has(e + 2):
                    after(pool, gather_idx, e + 2)
                    after(pool, rows_turned, e)
                    pool.sem_inc(waited, 1)
                    pool.indirect_dma_start(
                        out=s.rows[b][:].rearrange("p c q -> p (c q)"), out_offset=None, in_=s.xn2_rows,
                        in_offset=bass.IndirectOffsetOnAxis(ap=s.idx_g[b][:, 0:1], axis=0),
                        bounds_check=last_row, oob_is_err=False).then_inc(rows_in[b], 16)
                if last_down(e - 1, 5):
                    split_lo(pool, e, b, -1, 5)
                if has(e - 2):
                    after(pool, scatter_idx, e - 2)
                    for n in range(2):
                        after(pool, y_ready[n], e - 2)
                    pool.sem_inc(waited, 1)
                    pool.indirect_dma_start(
                        out=s.out_rows, out_offset=bass.IndirectOffsetOnAxis(ap=s.idx_s[b][:, 0:1], axis=0),
                        in_=s.y_sb[b][:], in_offset=None, bounds_check=last_row, oob_is_err=False,
                        compute_op=ALU.add).then_inc(scattered, 16)
                if not last_down(e - 1, 5):
                    split_lo(pool, e, b, -1, 5)
                if has(e - 2):
                    after(pool, scattered, e - 2, 16)
                    pool.sem_inc(y_free, 1)

            turns(turn)(pool)
            after(pool, scattered, E - 1, 16)

        @block.scalar
        def _(act):
            def turn(e, b, h):
                if last_down(e - 1, 4):
                    split_hi(act, e, b, h, -1, 4)
                    split_hi(act, e, b, h, -1, 5)
                if has(e - 2):
                    after(act, down_done, e - 2)
                    act.wait_ge(y_free, e - 1)
                    act.copy(s.y_sb[b][:, 0:512], ps[0:SLOTS, 2, :]).then_inc(y_ready[0], 1)
                if not last_down(e - 1, 4):
                    split_hi(act, e, b, h, -1, 4)
                    split_hi(act, e, b, h, 1, 0)
                    split_hi(act, e, b, h, -1, 5)
                if has(e - 1):
                    after(act, hid_turned, e - 1)
                    after(act, down_done, e - 2)
                    act.copy(s.hidT_hi[:], ps[:, 6, :].rearrange("p (c q) -> p c q", q=P)[:, :, 0:SLOTS]).then_inc(hT_hi_ready, 1)
                split_hi(act, e, b, h, 1, 1)
                split_hi(act, e, b, h, 1, 2)
                if has(e + 1):
                    after(act, rows_turned, e + 1)
                    after(act, gated, e - 1)
                    act.copy(as_banks(s.rT_hi[1 - b][:]), banks45).then_inc(rT_hi_ready, 1)
                split_hi(act, e, b, h, 1, 3)
                if has(e):
                    after(act, gated, e)
                    after(act, hid_ready, e - 1)
                    act.activation(s.silu[:], ps[0:SLOTS, 0, :], ACT.Silu).then_inc(silu_ready, 1)

            turns(turn)(act)

        @block.vector
        def _(dve):
            own = Order(dve, spare_steps)

            def turn(e, b, h):
                if isinstance(e, int) and e == 1:
                    dve.wait_ge(s.table_summed, 2)
                    spare_columns(dve, own.then, s, sp_tab)
                if last_down(e - 1, 4):
                    split_lo(dve, e, b, -1, 4)
                if has(e - 2):
                    after(dve, down_done, e - 2)
                    dve.wait_ge(y_free, e - 1)
                    dve.tensor_copy(s.idx_s[b][:], s.table[:, bass.ds(e - 2, 1), 0]).then_inc(scatter_idx, 1)
                    dve.tensor_copy(s.y_sb[b][:, 512:1024], ps[0:SLOTS, 3, :]).then_inc(y_ready[1], 1)
                if has(e + 2):
                    rows_loaded(dve, e, b, h, 0)
                    dve.tensor_copy(s.idx_g[b][:], s.table[:, bass.ds(e + 2, 1), 0]).then_inc(gather_idx, 1)
                if isinstance(e, int) and e == -1:
                    spare_places(dve, own.then, s, sp_tab)
                if isinstance(e, int) and e == 0:
                    spare_choices(dve, own.then, s, sp_tab)
                    spare_parts(dve, own.then, s, sp_tab)
                    dve.sem_inc(s.table_parts, 1)
                if not last_down(e - 1, 4):
                    split_lo(dve, e, b, -1, 4)
                split_lo(dve, e, b, 1, 0)
                if has(e - 1):
                    after(dve, hT_hi_ready, e - 1)
                    dve.tensor_tensor(s.hidT_lo[:], ps[:, 6, :].rearrange("p (c q) -> p c q", q=P)[:, :, 0:SLOTS],
                                      s.hidT_hi[:].bitcast(F32), ALU.subtract).then_inc(hT_lo_ready, 1)
                split_lo(dve, e, b, 1, 1)
                split_lo(dve, e, b, 1, 2)
                if has(e + 1):
                    after(dve, rT_hi_ready, e + 1)
                    dve.tensor_tensor(as_banks(s.rT_lo[1 - b][:]), banks45, as_banks(s.rT_hi[1 - b][:]).bitcast(F32),
                                      ALU.subtract).then_inc(rT_lo_ready, 1)
                split_lo(dve, e, b, 1, 3)
                if has(e):
                    after(dve, hid_ready, e - 2)
                    dve.tensor_copy(s.w_slot[b][:], s.table[:, bass.ds(e, 1), 1].bitcast(F32)).then_inc(weight_ready, 1)
                    after(dve, silu_ready, e)
                    after(dve, weight_ready, e)
                    after(dve, hid_turned, e - 2)
                    dve.scalar_tensor_tensor(s.hid[b][:].rearrange("s c p -> s p c"),
                                             s.silu[:].rearrange("s (p c) -> s p c", c=FC), s.w_slot[b][:],
                                             ps[0:SLOTS, 1, :].rearrange("s (p c) -> s p c", c=FC),
                                             ALU.mult, ALU.mult).then_inc(hid_ready, 1)

            turns(turn)(dve)

        @block.tensor
        def _(pe):
            def gate_up(e, b, q):
                if not has(e):
                    return
                if q == 0:
                    after(pe, rT_lo_ready, e)
                    after(pe, hid_ready, e - 1)
                after(pe, s.lo_ready[q], e)
                hi = s.w_hi[q][:].rearrange("p (g c n) -> p g c n", g=2, c=2)
                lo = s.w_lo[b][q][:].rearrange("p (g c n) -> p g c n", g=2, c=2)
                for c2 in range(2):
                    c = 2 * q + c2
                    for g in range(2):
                        pe.matmul(ps[0:SLOTS, g, :], s.rT_hi[b][:, c, :], hi[:, g, c2, :], start=(c == 0), stop=False)
                    for g in range(2):
                        pe.matmul(ps[0:SLOTS, g, :], s.rT_hi[b][:, c, :], lo[:, g, c2, :], start=False, stop=False)
                    for g in range(2):
                        ins = pe.matmul(ps[0:SLOTS, g, :], s.rT_lo[b][:, c, :], hi[:, g, c2, :], start=False, stop=(c == KC - 1))
                ins.then_inc(used[q], 1)
                if q == 3:
                    pe.wait_ge(used[q], (e + 1))
                    pe.sem_inc(gated, 1)

            def down(e, b, q):
                if not has(e):
                    return
                if q == 0:
                    after(pe, hT_lo_ready, e)
                    for n in range(2):
                        after(pe, y_ready[n], e - 1)
                after(pe, s.lo_ready[4 + q], e)
                hi = hi_of(e, 4 + q)[:].rearrange("p (c n) -> p c n", c=2)
                lo = s.w_lo[b][4 + q][:].rearrange("p (c n) -> p c n", c=2)
                for c2 in range(2):
                    c = 2 * q + c2
                    for n in range(2):
                        pe.matmul(ps[0:SLOTS, 2 + n, :], s.hidT_hi[:, c, :], hi[:, c2, n * 512:(n + 1) * 512], start=(c == 0), stop=False)
                    for n in range(2):
                        pe.matmul(ps[0:SLOTS, 2 + n, :], s.hidT_hi[:, c, :], lo[:, c2, n * 512:(n + 1) * 512], start=False, stop=False)
                    for n in range(2):
                        ins = pe.matmul(ps[0:SLOTS, 2 + n, :], s.hidT_lo[:, c, :], hi[:, c2, n * 512:(n + 1) * 512], start=False, stop=(c == FC - 1))
                ins.then_inc(used[4 + q], 1)
                if q == 1:
                    pe.wait_ge(used[4 + q], (e + 1))
                    pe.sem_inc(down_done, 1)

            def turn(e, b, h):
                gate_up(e, b, 0)
                gate_up(e, b, 1)
                if has(e - 1):
                    after(pe, hid_ready, e - 1)
                    after(pe, hT_lo_ready, e - 2)
                    for c in range(FC):
                        ins = pe.transpose(ps[:, 6, c * P:c * P + SLOTS], s.hid[1 - b][:, c, :], s.ident[0:SLOTS, 0:SLOTS])
                    ins.then_inc(hid_turned, 1)
                gate_up(e, b, 2)
                if has(e + 1):
                    rows_loaded(pe, e, b, h, 1)
                    after(pe, rT_lo_ready, e)
                    for c in range(KC):
                        ins = pe.transpose(ps[:, 4 + c // 4, (c % 4) * P:(c % 4) * P + SLOTS], s.rows[1 - b][:, c, :], s.ident[0:SLOTS, 0:SLOTS])
                    ins.then_inc(rows_turned, 1)
                gate_up(e, b, 3)
                if isinstance(e, int) and e == 0:
                    pe.wait_ge(s.table_parts, 2)
                    for j in range(TOP_K * NT):
                        ins = pe.matmul(ps[0:SLOTS, 7, 0:2 * SPARE], sp_tab.in_slot[:, j, :],
                                        sp_tab.entry[:, j, :, :].rearrange("p a b -> p (a b)"),
                                        start=(j == 0), stop=(j == TOP_K * NT - 1))
                    ins.then_inc(s.table_summed, 1)
                down(e - 1, 1 - b, 0)
                down(e - 1, 1 - b, 1)

            turns(turn)(pe)

    x = Shared()
    x.scattered, x.gather_idx, x.waited, x.rows_in, x.y_ready = scattered, gather_idx, waited, rows_in, y_ready
    x.gated, x.silu_ready, x.weight_ready, x.rows_turned, x.rT_hi_ready = gated, silu_ready, weight_ready, rows_turned, rT_hi_ready
    x.hid_ready, x.hid_turned, x.hT_hi_ready, x.down_done = hid_ready, hid_turned, hT_hi_ready, down_done
    spare_blocks(nc, s, x)


def spare_blocks(nc, s, x):
    ps = s.ps

    def each(eng, body):
        n = eng.value_load(s.spare_n[0:1, 0:1], min_val=0, max_val=SPARE)
        with eng.If(n > 0):
            with eng.Fori(0, SPARE) as i:
                with eng.If(n > i):
                    body(i)
            eng.nop()
        eng.nop()

    def before_done(eng, i):
        eng.wait_ge(x.scattered, i * 16 + E * 16)

    with nc.Block() as block:
        @block.sync
        def _(sp):
            def body(i):
                before_done(sp, i)
                e = sp.value_load(s.spare_e[0:1, bass.ds(i, 1)], min_val=0, max_val=E - 1)
                for q in range(4):
                    s.load_gate_up(sp, e, 0, q)
                for q in range(2):
                    s.load_down(sp, e, 0, q)

            each(sp, body)

        @block.gpsimd
        def _(pool):
            last_row = pool.to_reg(T - 1)

            def body(i):
                pool.wait_ge(x.gather_idx, i + (E + 1))
                pool.sem_inc(x.waited, 1)
                pool.indirect_dma_start(
                    out=s.rows[0][:].rearrange("p c q -> p (c q)"), out_offset=None, in_=s.xn2_rows,
                    in_offset=bass.IndirectOffsetOnAxis(ap=s.idx_g[0][:, 0:1], axis=0),
                    bounds_check=last_row, oob_is_err=False).then_inc(x.rows_in[0], 16)
                pool.wait_ge(x.y_ready[0], i + (E + 1))
                pool.sem_inc(x.waited, 1)
                pool.indirect_dma_start(
                    out=s.out_rows, out_offset=bass.IndirectOffsetOnAxis(ap=s.idx_g[0][:, 0:1], axis=0),
                    in_=s.y_sb[0][:], in_offset=None, bounds_check=last_row, oob_is_err=False,
                    compute_op=ALU.add).then_inc(x.scattered, 16)
                before_done(pool, i + 1)

            each(pool, body)

        @block.scalar
        def _(act):
            def body(i):
                act.wait_ge(x.gated, i + (E + 1))
                act.activation(s.silu[:], ps[0:SLOTS, 0, :], ACT.Silu).then_inc(x.silu_ready, 1)

            each(act, body)

        @block.vector
        def _(dve):
            def body(i):
                before_done(dve, i)
                dve.tensor_copy(s.idx_g[0][:], s.table[:, bass.ds(i + E, 1), 0]).then_inc(x.gather_idx, 1)
                dve.tensor_copy(s.w_slot[0][:], s.table[:, bass.ds(i + E, 1), 1].bitcast(F32)).then_inc(x.weight_ready, 1)
                dve.wait_ge(x.rows_turned, i + (E + 1))
                dve.tensor_copy(s.spare_xT[:].rearrange("p (a c) q -> p a c q", a=2),
                                ps[:, 4:6, :].rearrange("p a (c q) -> p a c q", q=P)[:, :, :, 0:SLOTS]).then_inc(x.rT_hi_ready, 1)
                dve.wait_ge(x.silu_ready, i + (E + 1))
                dve.wait_ge(x.weight_ready, i + (E + 1))
                dve.scalar_tensor_tensor(s.hid[0][:].rearrange("s c p -> s p c"),
                                         s.silu[:].rearrange("s (p c) -> s p c", c=FC), s.w_slot[0][:],
                                         ps[0:SLOTS, 1, :].rearrange("s (p c) -> s p c", c=FC),
                                         ALU.mult, ALU.mult).then_inc(x.hid_ready, 1)
                dve.wait_ge(x.hid_turned, i + (E + 1))
                dve.tensor_copy(s.spare_hT[:], ps[:, 6, :].rearrange("p (c q) -> p c q", q=P)[:, :, 0:SLOTS]).then_inc(x.hT_hi_ready, 1)
                dve.wait_ge(x.down_done, i + (E + 1))
                dve.tensor_copy(s.y_sb[0][:].rearrange("p (a n) -> p a n", a=2), ps[0:SLOTS, 2:4, :]).then_inc(x.y_ready[0], 1)

            each(dve, body)

        @block.tensor
        def _(pe):
            def body(i):
                pe.wait_ge(x.rows_in[0], i * 16 + 16 * (E // 2 + 1))
                for c in range(KC):
                    ins = pe.transpose(ps[:, 4 + c // 4, (c % 4) * P:(c % 4) * P + SLOTS], s.rows[0][:, c, :], s.ident[0:SLOTS, 0:SLOTS])
                ins.then_inc(x.rows_turned, 1)
                pe.wait_ge(x.rT_hi_ready, i + (E + 1))
                for c in range(KC):
                    pe.wait_ge(s.loaded[0][c // 2], i * 32 + 32 * (E // 2 + 1))
                    w = s.raw[0][c // 2][:].rearrange("p (g c n) -> p g c n", g=2, c=2)
                    for g in range(2):
                        ins = pe.matmul(ps[0:SLOTS, g, :], s.spare_xT[:, c, :], w[:, g, c % 2, :], start=(c == 0), stop=(c == KC - 1))
                ins.then_inc(x.gated, 1)
                pe.wait_ge(x.hid_ready, i + (E + 1))
                for c in range(FC):
                    ins = pe.transpose(ps[:, 6, c * P:c * P + SLOTS], s.hid[0][:, c, :], s.ident[0:SLOTS, 0:SLOTS])
                ins.then_inc(x.hid_turned, 1)
                pe.wait_ge(x.hT_hi_ready, i + (E + 1))
                for c in range(FC):
                    pe.wait_ge(s.loaded[0][4 + c // 2], i * 16 + 16 * (E // 2 + 1))
                    w = s.raw[0][4 + c // 2][:].rearrange("p (c n) -> p c n", c=2)
                    for n in range(2):
                        ins = pe.matmul(ps[0:SLOTS, 2 + n, :], s.spare_hT[:, c, :], w[:, c % 2, n * 512:(n + 1) * 512],
                                        start=(c == 0), stop=(c == FC - 1))
                ins.then_inc(x.down_done, 1)

            each(pe, body)


_INS = ["x", "positions", "attn_norm_gain", "w_in", "q_norm_gain", "k_norm_gain", "lambda_q1",
        "lambda_k1", "lambda_q2", "lambda_k2", "subln_gain", "conv_w", "conv_out_gain", "w_out",
        "ffn_norm_gain", "w_group_router", "w_expert_router", "w_gate", "w_up", "w_down"]


def kernel(**inputs):
    import numpy as _np
    import concourse.bacc as _bacc
    from concourse import mybir as _mybir
    from concourse.bass_utils import run_bass_kernel_spmd as _run

    nc = _bacc.Bacc("TRN2", target_bir_lowering=False, num_devices=1)
    arrays, args = {}, []
    for name in _INS:
        a = _np.ascontiguousarray(inputs[name])
        arrays[f"in_{name}"] = a
        args.append(nc.dram_tensor(f"in_{name}", a.shape, _mybir.dt.from_np(a.dtype), kind="ExternalInput").ap())
    args.append(nc.dram_tensor("out_0", (1, T, D), _mybir.dt.float32, kind="ExternalOutput").ap())
    layer_kernel(nc, *args)
    r = _run(nc, [arrays], core_ids=[0])
    return r.results[0]["out_0"]
```
